# Optimizing a Trainium2 kernel written in Bass

```python
import jax, jax.numpy as jnp
from jax import lax
import numpy as np

D_MODEL = 1024
BATCH = 1
SEQ = 512
DEPTH = 1

GRID_W = 64
HEAD_DIM = 64
ATTN_HEADS = 8
ATTN_KV_HEADS = 2
ATTN_GROUP = ATTN_HEADS // ATTN_KV_HEADS
ROPE_THETA = 10000.0
Q_BLOCK = 128
HGRN_HEADS = 8
HGRN_KEY_DIM = 64
HGRN_VAL_DIM = 64
HGRN_CHUNK = 32
ATTN_WIDTH = ATTN_HEADS * HEAD_DIM
KV_WIDTH = ATTN_KV_HEADS * HEAD_DIM
HGRN_KW = HGRN_HEADS * HGRN_KEY_DIM
HGRN_VW = HGRN_HEADS * HGRN_VAL_DIM
D_FF = 2816
NORM_EPS = 1e-6
IN_SPLITS = (ATTN_WIDTH, KV_WIDTH, KV_WIDTH, HGRN_KW, HGRN_KW, HGRN_KW, HGRN_VW, HGRN_VW, D_MODEL, D_MODEL)
IN_WIDTH = 3 * KV_WIDTH + ATTN_WIDTH - KV_WIDTH + 3 * HGRN_KW + 2 * HGRN_VW + 2 * D_MODEL

kernel_name = "hybrid_gqa_axial_hgrn2_macaron"

def rmsnorm(x, g):
    x32 = x.astype(jnp.float32)
    y = x32 * lax.rsqrt(jnp.mean(x32 * x32, axis=-1, keepdims=True) + NORM_EPS)
    return (y * g.astype(jnp.float32)).astype(x.dtype)

def swiglu(h, w_gate, w_up, w_down):
    return (jax.nn.silu(h @ w_gate) * (h @ w_up)) @ w_down

def split_columns(p):
    offsets = [int(o) for o in np.cumsum(IN_SPLITS)[:-1]]
    return jnp.split(p, offsets, axis=-1)

def axial_rope_tables(seq_len):
    rows = seq_len // GRID_W
    row = jnp.repeat(jnp.arange(rows, dtype=jnp.float32), GRID_W)
    col = jnp.tile(jnp.arange(GRID_W, dtype=jnp.float32), rows)
    n_freq = HEAD_DIM // 4
    inv = ROPE_THETA ** (-jnp.arange(n_freq, dtype=jnp.float32) / n_freq)
    ang = jnp.concatenate([row[:, None] * inv, col[:, None] * inv], axis=-1)
    return jnp.cos(ang), jnp.sin(ang)

def apply_rope(x, cos, sin):
    x32 = x.astype(jnp.float32)
    x1, x2 = jnp.split(x32, 2, axis=-1)
    c = cos[:, None, :]
    s = sin[:, None, :]
    return jnp.concatenate([x1 * c - x2 * s, x2 * c + x1 * s], axis=-1).astype(x.dtype)

def axial_gqa_attention(q, k, v, q_g, k_g, cos, sin):
    B, S, _ = q.shape
    q = apply_rope(rmsnorm(q.reshape(B, S, ATTN_HEADS, HEAD_DIM), q_g), cos, sin)
    k = apply_rope(rmsnorm(k.reshape(B, S, ATTN_KV_HEADS, HEAD_DIM), k_g), cos, sin)
    v = v.reshape(B, S, ATTN_KV_HEADS, HEAD_DIM)
    q = (q * (HEAD_DIM ** -0.5)).reshape(B, S // Q_BLOCK, Q_BLOCK, ATTN_KV_HEADS, ATTN_GROUP, HEAD_DIM)
    q_blocks = jnp.moveaxis(q, 1, 0)

    def attend(qb):
        s = jnp.einsum('bqgrd,bkgd->bgrqk', qb, k).astype(jnp.float32)
        p = jax.nn.softmax(s, axis=-1).astype(v.dtype)
        return jnp.einsum('bgrqk,bkgd->bqgrd', p, v)

    o = lax.map(attend, q_blocks)
    return jnp.moveaxis(o, 0, 1).reshape(B, S, ATTN_WIDTH)

def gated_scan_chunked(q, k, v, log_f):
    B, H, S, Dk = q.shape
    Dv = v.shape[-1]
    C = HGRN_CHUNK
    N = S // C
    q, k, v, log_f = [t.astype(jnp.float32).reshape(B, H, N, C, t.shape[-1]) for t in (q, k, v, log_f)]
    b = jnp.cumsum(log_f, axis=3)
    b_mid = b[:, :, :, C // 2 - 1:C // 2, :]
    b_last = b[:, :, :, C - 1:, :]
    scores = jnp.einsum('bhntd,bhnsd->bhnts', q * jnp.exp(b - b_mid), k * jnp.exp(b_mid - b))
    lower = jnp.tril(jnp.ones((C, C), dtype=bool))
    scores = jnp.where(lower, scores, 0.0)
    o_intra = jnp.einsum('bhnts,bhnse->bhnte', scores, v)
    contrib = jnp.einsum('bhnsd,bhnse->bhnde', k * jnp.exp(b_last - b), v)
    decay = jnp.exp(b_last[:, :, :, 0, :])

    def step(state, inp):
        dec, add = inp
        return dec[..., None] * state + add, state

    _, states_in = lax.scan(step, jnp.zeros((B, H, Dk, Dv), jnp.float32),
                            (jnp.moveaxis(decay, 2, 0), jnp.moveaxis(contrib, 2, 0)))
    states_in = jnp.moveaxis(states_in, 0, 2)
    o_inter = jnp.einsum('bhntd,bhnde->bhnte', q * jnp.exp(b), states_in)
    return (o_intra + o_inter).reshape(B, H, S, Dv)

def hgrn2_bidirectional(q, f_fwd, f_bwd, i, g, lb, norm_g):
    B, S, _ = q.shape

    def heads(t, d):
        return t.reshape(B, S, HGRN_HEADS, d).transpose(0, 2, 1, 3)

    qh = heads(jax.nn.silu(q), HGRN_KEY_DIM)
    vh = heads(i, HGRN_VAL_DIM)

    def direction(f_logits, lb_dir, reverse):
        f = lb_dir + (1.0 - lb_dir) * jax.nn.sigmoid(f_logits.astype(jnp.float32))
        kh = heads(1.0 - f, HGRN_KEY_DIM)
        lfh = heads(jnp.log(f), HGRN_KEY_DIM)
        ts = (qh, kh, vh, lfh)
        if reverse:
            ts = tuple(jnp.flip(t, axis=2) for t in ts)
        o = gated_scan_chunked(*ts)
        return jnp.flip(o, axis=2) if reverse else o

    o = direction(f_fwd, lb[0], False) + direction(f_bwd, lb[1], True)
    o = rmsnorm(o.transpose(0, 2, 1, 3), norm_g.reshape(HGRN_HEADS, HGRN_VAL_DIM))
    o = o.reshape(B, S, HGRN_VW) * jax.nn.silu(g.astype(jnp.float32))
    return o.astype(g.dtype)

def setup_inputs(seed: int = 0) -> dict:
    key = jax.random.key(seed)
    ks = jax.random.split(key, 20)
    f32 = jnp.float32

    def w(k, shape, fan_in):
        return jax.random.normal(k, shape, f32) * (fan_in ** -0.5)

    def gain(k, shape):
        return 1.0 + 0.02 * jax.random.normal(k, shape, f32)

    return {
        "x": jax.random.normal(ks[0], (BATCH, SEQ, D_MODEL), f32),
        "ffn1_norm_g": gain(ks[1], (DEPTH, D_MODEL)),
        "ffn1_w_gate": w(ks[2], (DEPTH, D_MODEL, D_FF), D_MODEL),
        "ffn1_w_up": w(ks[3], (DEPTH, D_MODEL, D_FF), D_MODEL),
        "ffn1_w_down": w(ks[4], (DEPTH, D_FF, D_MODEL), D_FF),
        "mix_norm_g": gain(ks[5], (DEPTH, D_MODEL)),
        "w_in": w(ks[6], (DEPTH, D_MODEL, IN_WIDTH), D_MODEL),
        "q_norm_g": gain(ks[7], (DEPTH, HEAD_DIM)),
        "k_norm_g": gain(ks[8], (DEPTH, HEAD_DIM)),
        "hgrn_lb_logits": 0.1 * jax.random.normal(ks[9], (2, DEPTH + 1, HGRN_KW), f32),
        "hgrn_out_norm_g": gain(ks[10], (DEPTH, HGRN_VW)),
        "w_branch_attn": w(ks[11], (DEPTH, ATTN_WIDTH, D_MODEL), ATTN_WIDTH),
        "w_branch_hgrn": w(ks[12], (DEPTH, HGRN_VW, D_MODEL), HGRN_VW),
        "w_out": w(ks[13], (DEPTH, D_MODEL, D_MODEL), D_MODEL),
        "ffn2_norm_g": gain(ks[14], (DEPTH, D_MODEL)),
        "ffn2_w_gate": w(ks[15], (DEPTH, D_MODEL, D_FF), D_MODEL),
        "ffn2_w_up": w(ks[16], (DEPTH, D_MODEL, D_FF), D_MODEL),
        "ffn2_w_down": w(ks[17], (DEPTH, D_FF, D_MODEL), D_FF),
        "final_norm_g": gain(ks[18], (D_MODEL,)),
    }

def reference(x, ffn1_norm_g, ffn1_w_gate, ffn1_w_up, ffn1_w_down, mix_norm_g, w_in,
              q_norm_g, k_norm_g, hgrn_lb_logits, hgrn_out_norm_g, w_branch_attn,
              w_branch_hgrn, w_out, ffn2_norm_g, ffn2_w_gate, ffn2_w_up, ffn2_w_down,
              final_norm_g):
    S = x.shape[1]
    cos, sin = axial_rope_tables(S)
    lb_all = jnp.cumsum(jax.nn.softmax(hgrn_lb_logits.astype(jnp.float32), axis=1), axis=1)
    for l in range(DEPTH):
        x = x + 0.5 * swiglu(rmsnorm(x, ffn1_norm_g[l]), ffn1_w_gate[l], ffn1_w_up[l], ffn1_w_down[l])
        h = rmsnorm(x, mix_norm_g[l])
        aq, ak, av, hq, hff, hfb, hi, hg, ga, gb = split_columns(h @ w_in[l])
        y_attn = axial_gqa_attention(aq, ak, av, q_norm_g[l], k_norm_g[l], cos, sin) @ w_branch_attn[l]
        y_hgrn = hgrn2_bidirectional(hq, hff, hfb, hi, hg, lb_all[:, l, :], hgrn_out_norm_g[l]) @ w_branch_hgrn[l]
        merged = jax.nn.sigmoid(ga) * y_attn + jax.nn.sigmoid(gb) * y_hgrn
        x = x + merged @ w_out[l]
        x = x + 0.5 * swiglu(rmsnorm(x, ffn2_norm_g[l]), ffn2_w_gate[l], ffn2_w_up[l], ffn2_w_down[l])
    return rmsnorm(x, final_norm_g)


_drawn_inputs = setup_inputs


def setup_inputs(seed=0):
    import zlib

    import numpy as np

    out = dict(_drawn_inputs(seed))
    spreads = {}
    factors = {'ffn1_norm_g': 5.869,
     'mix_norm_g': 5.759,
     'q_norm_g': 8.0,
     'k_norm_g': 8.0,
     'hgrn_lb_logits': 8.0,
     'hgrn_out_norm_g': 8.0,
     'ffn2_norm_g': 7.548,
     'final_norm_g': 2.91}
    for name, (base, spread) in spreads.items():
        noise = np.random.default_rng([zlib.crc32(name.encode()), seed]).standard_normal(out[name].shape)
        drawn = base * np.exp(spread * noise) if base else spread * noise
        out[name] = __import__('jax').numpy.asarray(drawn.astype(out[name].dtype))
    for name, factor in factors.items():
        out[name] = (out[name] * factor).astype(out[name].dtype)
    return out
```

```python
from contextlib import ExitStack

import numpy as np

import concourse.bass as bass
from concourse import mybir

F32 = mybir.dt.float32
F32R = mybir.dt.float32r
I32 = mybir.dt.int32
U32 = mybir.dt.uint32
ALU = mybir.AluOpType
ACT = mybir.ActivationFunctionType
AX = mybir.AxisListType

P = 128
D, S, FF = 1024, 512, 2816
HD = 64
NH, NKV = 8, 2
HH = 8
CHUNK = 32
NCH = S // CHUNK
EPS = 1e-6
KT = D // P
FT = FF // P
ST = S // P
UW = KT * P
DW = FT // 2 * P
RAW_SLOTS, W_SLOTS, AHEAD = 2, 4, 3
PAIRS = HH // 2

STREAMS = [("up1", 2 * FT, UW), ("down1", 2 * KT, DW), ("proj", 26, UW), ("merge", 3 * KT, UW),
           ("wout", KT, UW), ("up2", 2 * FT, UW), ("down2", 2 * KT, DW)]
BASE, WIDTH = {}, []
for _name, _count, _width in STREAMS:
    BASE[_name] = len(WIDTH)
    WIDTH += [_width] * _count
UNITS = len(WIDTH)

PROJ = ([("av", 0), ("ak", 0)] + [("aq", t) for t in range(4)] + [("hi", t) for t in range(4)]
        + [("hf", h) for h in range(HH)] + [("hq", t) for t in range(4)] + [("hg", t) for t in range(4)])
V_TILES = {i: w for w, i in enumerate(i for i, (kind, _) in enumerate(PROJ) if kind in ("av", "hi"))}
FIRST_ITEM = 10
ITEMS = 4 * ST

MIX_CONSTS = [("cos", S), ("sin", S), ("keep", S), ("mask", 2 * P), ("head_mean", P), ("swap", P)]
MIX_COLS = sum(w for _, w in MIX_CONSTS)


def build(nc, xT_in, up1, down1, proj, merge, wout, up2, down2, mix_const, small_const, gains, lb_logits, outT):
    with ExitStack() as ctx:
        def sb(name, shape, dt=F32):
            return ctx.enter_context(nc.sbuf_tensor(name, shape, dt))

        def sem(name):
            return ctx.enter_context(nc.semaphore(name))

        xT = sb("xT", [P, KT, S])
        h_hi, h_lo = sb("h_hi", [P, KT, S], F32R), sb("h_lo", [P, KT, S], F32R)
        raw = sb("raw", [P, RAW_SLOTS, DW])
        w_hi, w_lo = sb("w_hi", [P, W_SLOTS, DW], F32R), sb("w_lo", [P, W_SLOTS, DW], F32R)
        rs = sb("rs", [P, S])
        sq_sum = sb("sq_sum", [P, S])
        sq = sb("sq", [P, S])
        small = sb("small", [P, 2 * P])
        ones, ident = small[:, 0:P], small[:, P:2 * P]
        norm_v, norm_y, norm_t = (sb(n, [P, ST]) for n in ("norm_v", "norm_y", "norm_t"))
        gain = sb("gain", [P, 42])
        gq8 = sb("gq8", [P, 1])
        lbl = sb("lbl", [P, 2, HH])
        lb, one_minus_lb = sb("lb", [P, HH]), sb("one_minus_lb", [P, HH])
        lbt = sb("lbt", [P, 2, HH])
        neg_max, prob_sum = sb("neg_max", [P, ITEMS, 2]), sb("prob_sum", [P, ITEMS, 2])
        inv_sum = sb("inv_sum", [P, 2])
        b_mid, b_last, decay = sb("b_mid", [P, NCH]), sb("b_last", [P, NCH]), sb("decay", [P, 2, NCH])

        REGION = 96 * 1024
        region_at = nc.sbuf_base
        sb("region", [P, REGION // 4])
        ffn_words = 2 * FT * S

        def at(name, kib, shape, dt=F32):
            n = 4 * int(np.prod(shape[1:]))
            assert kib * 1024 + n <= REGION, name
            return nc.alloc_sbuf_tensor_at(name, shape, dt, offset=region_at + int(kib * 1024))

        assert ffn_words * 4 <= 88 * 1024
        g_hi, g_lo = at("g_hi", 0, [P, FT, S], F32R), at("g_lo", 44, [P, FT, S], F32R)
        gn, sg, un = at("gn", 88, [P, S]), at("sg", 90, [P, S]), at("un", 92, [P, S])

        forget = at("forget", 0, [P, HH, S])
        yb = at("yb", 0, [P, 2 * PAIRS, S], F32R)
        ya_hi, ya_lo = at("ya_hi", 16, [P, 4, S], F32R), at("ya_lo", 24, [P, 4, S], F32R)
        hq, hgate = at("hq", 32, [P, 4, S]), at("hgate", 40, [P, 4, S])
        v_h = at("v_h", 48, [P, ST, S])
        consts = at("consts", 56, [P, MIX_COLS])
        c = {}
        col = 0
        for name, width in MIX_CONSTS:
            c[name] = consts[:, col:col + width]
            col += width
        qk = at("qk", 64, [P, 5, S])
        v_a = at("v_a", 74, [P, ST, P])
        prob = at("prob", 76, [P, 2, S])
        prob_t = at("prob_t", 80, [P, 2, ST, P])
        y_nat = at("y_nat", 84, [P, 2, P])
        v_tmp = at("v_tmp", 85, [P, S])
        q_sq, q_ms, q_rs, q_t = (at(n, 87 + 2 * i, [P, S]) for i, n in enumerate(("q_sq", "q_ms", "q_rs", "q_t")))
        k_in = [at("k_in0", 64, [P, S]), sq_sum]
        b_cum = [at("b_cum0", 66, [P, S]), at("b_cum1", 68, [P, S])]
        k_sc = [at("k_sc0", 70, [P, S]), at("k_sc1", 72, [P, S])]
        q_sc, k_end, q_dup = at("q_sc", 74, [P, S]), at("k_end", 76, [P, S]), at("q_dup", 78, [P, S])
        k_nat = sq
        sc_m = at("sc_m", 80, [P, 2, S])
        state = at("state", 84, [P, NCH, HD])
        v_exp = at("v_exp", 88, [P, ST, 4, HD])
        o_ms, o_rs = at("o_ms", 92, [P, S]), at("o_rs", 94, [P, S])
        o_t = at("o_t", 56, [P, S])
        o_u = at("o_u", 58, [P, S])
        m_hi, m_lo = at("m_hi", 32, [P, KT, S], F32R), at("m_lo", 48, [P, KT, S], F32R)
        sga, sgb = at("sga", 64, [P, S]), at("sgb", 66, [P, S])

        ps = ctx.enter_context(nc.psum_tensor("ps", [P, 8, S], F32))
        UP_BANKS, RES_BANKS, MEAN_BANK = (0, 2), 4, 6

        raw_loaded = [sem(f"raw_loaded{i}") for i in range(RAW_SLOTS)]
        x_loaded = [sem(f"x_loaded{n}") for n in range(KT)]
        const_loaded, small_loaded, mix_loaded = sem("const_loaded"), sem("small_loaded"), sem("mix_loaded")
        hi_done, lo_done, unit_done = sem("hi_done"), sem("lo_done"), sem("unit_done")
        x_done, sq_done, sum_done = sem("x_done"), sem("sq_done"), sem("sum_done")
        hh_done, h_done, mean_done = sem("hh_done"), sem("h_done"), sem("mean_done")
        diag_done, spread_done, rs_done = sem("diag_done"), sem("spread_done"), sem("rs_done")
        gate_read, up_read, sig_done = sem("gate_read"), sem("up_read"), sem("sig_done")
        prod_done, act_done, ghi_done, glo_done = sem("prod_done"), sem("act_done"), sem("ghi_done"), sem("glo_done")
        dve_seq, act_seq, pool_seq = sem("dve_seq"), sem("act_seq"), sem("pool_seq")
        lb_loaded, lb_exp, lb_ready = sem("lb_loaded"), sem("lb_exp"), sem("lb_ready")
        proj_read = sem("proj_read")
        vt_done, vn_done = sem("vt_done"), sem("vn_done")
        qsq_done, qms_done, qeps_done, qr_done = sem("qsq_done"), sem("qms_done"), sem("qeps_done"), sem("qr_done")
        qn_done, qswap_done, rope_done = sem("qn_done"), sem("qswap_done"), sem("rope_done")
        s_done, nm_done, p_done, pt_done = sem("s_done"), sem("nm_done"), sem("p_done"), sem("pt_done")
        pta_done, ptb_done, pv_done, yn_done = sem("pta_done"), sem("ptb_done"), sem("pv_done"), sem("yn_done")
        yt_done, yahi_done, yalo_done = sem("yt_done"), sem("yahi_done"), sem("yalo_done")
        fs_done, sl_done, sil_done = sem("fs_done"), sem("sl_done"), sem("sil_done")
        f_done, k_done, lf_done, b_done = sem("f_done"), sem("k_done"), sem("lf_done"), sem("b_done")
        d1_done, d3_done, bl_done = sem("d1_done"), sem("d3_done"), sem("bl_done")
        e1_done, e2_done, e3_done, e4_done = sem("e1_done"), sem("e2_done"), sem("e3_done"), sem("e4_done")
        qs_done, ks_done, ke_done, qe_done = sem("qs_done"), sem("ks_done"), sem("ke_done"), sem("qe_done")
        sc_done, scm_done, kt_done, kn_done = sem("sc_done"), sem("scm_done"), sem("kt_done"), sem("kn_done")
        zero_done, vexp_done, con_done, state_done = sem("zero_done"), sem("vexp_done"), sem("con_done"), sem("state_done")
        o_done, ocopy_done, osq_done, oms_done = sem("o_done"), sem("ocopy_done"), sem("osq_done"), sem("oms_done")
        oeps_done, or_done, on_done, ybhi_done, yblo_done = (sem(n) for n in (
            "oeps_done", "or_done", "on_done", "ybhi_done", "yblo_done"))
        ga_read, gb_read, sga_done, sgb_done = sem("ga_read"), sem("gb_read"), sem("sga_done"), sem("sgb_done")
        br_read, m_done, mhi_done, mlo_done = sem("br_read"), sem("m_done"), sem("mhi_done"), sem("mlo_done")
        scaled, out_dve, out_pool, out_stored = sem("scaled"), sem("out_dve"), sem("out_pool"), sem("out_stored")
        POOL_OUT = (5, 6, 7)
        RAW_CREDIT, W_CREDIT, BANK_CREDIT = RAW_SLOTS, W_SLOTS, 2

        block = ctx.enter_context(nc.Block())
        last = UNITS - 1

        @block.sync
        def _(sp):
            for name, count, width in STREAMS:
                src, base = dict(up1=up1, down1=down1, proj=proj, merge=merge, wout=wout, up2=up2, down2=down2)[name], BASE[name]
                with sp.Fori(0, count // 2) as it:
                    for i in range(2):
                        sp.wait_ge(lo_done, 2 * it + base + i + 1)
                        sp.dma_start(raw[:, i, 0:width], src[2 * it + i, :, :]).then_inc(raw_loaded[i], 16)
            for n in (0, 1, 5, 2, 3, 6, 4, 7):
                if n in POOL_OUT:
                    sp.wait_ge(out_pool, n - POOL_OUT[0] + 1)
                else:
                    sp.wait_ge(out_dve, n + 1)
                sp.dma_start(outT[:, n, :], xT[:, n, :]).then_inc(out_stored, 16)
            sp.wait_ge(out_stored, 16 * KT)

        @block.gpsimd
        def _(pool):
            def accumulate(first, n_of, a):
                pool.wait_ge(sq_done, a + 1)
                if first:
                    nc.gpsimd.tensor_copy(sq_sum[:], sq[:]).then_inc(sum_done, 1)
                else:
                    pool.wait_ge(sum_done, a)
                    nc.gpsimd.tensor_tensor(sq_sum[:], sq_sum[:], sq[:], ALU.add).then_inc(sum_done, 1)

            for r in range(2):
                if r:
                    pool.wait_ge(mean_done, r)
                for n in range(KT):
                    accumulate(n == 0, n, 8 * r + n)
            pool.wait_ge(yalo_done, 4)
            pool.wait_ge(pv_done, ITEMS)
            nc.gpsimd.memset(sc_m[:], 0.0).then_inc(zero_done, 1)
            nc.gpsimd.memset(state[:], 0.0).then_inc(zero_done, 1)
            pool.wait_ge(zero_done, 2)
            pool.wait_ge(vn_done, 5)

            def key(h):
                pool.wait_ge(f_done, h + 1)
                if h >= 2:
                    pool.wait_ge(ks_done, h - 1)
                nc.gpsimd.tensor_scalar(k_in[h % 2][:], forget[:, h, :], -1.0, 1.0, ALU.mult, ALU.add).then_inc(k_done, 1)

            def to_end(h):
                pool.wait_ge(bl_done, h + 1)
                if h >= 1:
                    pool.wait_ge(kt_done, h)
                chunks = lambda t: t[:].rearrange("p (n c) -> p n c", c=CHUNK)
                nc.gpsimd.tensor_tensor(chunks(k_end), b_last[:].unsqueeze(2).to_broadcast([P, NCH, CHUNK]), chunks(b_cum[h % 2]),
                                        ALU.subtract).then_inc(d3_done, 1)

            key(0)
            to_end(0)
            for h in range(HH):
                if h + 1 < HH:
                    key(h + 1)
                pool.wait_ge(e3_done, h + 1)
                nc.gpsimd.tensor_tensor(k_end[:], k_end[:], k_in[h % 2][:], ALU.mult).then_inc(ke_done, 1)
                if h >= 1:
                    pool.wait_ge(con_done, h)
                for j in range(4):
                    ins = nc.gpsimd.tensor_scalar(v_exp[:, :, j, :], v_h[:, :, HD * h:HD * (h + 1)], gain[:, 38 + j:39 + j], None, ALU.mult)
                ins.then_inc(vexp_done, 1)
                if h + 1 < HH:
                    to_end(h + 1)
            for r in range(2, 4):
                pool.wait_ge(mean_done, r)
                for n in range(KT):
                    accumulate(n == 0, n, 8 * r + n)
            for i, n in enumerate(POOL_OUT):
                pool.wait_ge(rs_done, 4)
                pool.wait_ge(scaled, n + 1)
                nc.gpsimd.tensor_tensor(xT[:, n, :], xT[:, n, :], rs[:], ALU.mult).then_inc(out_pool, 1)

        @block.scalar
        def _(act):
            A = nc.scalar.activation
            act.dma_start(gain[:], gains).then_inc(const_loaded, 16)
            act.dma_start(small[:], small_const).then_inc(small_loaded, 16)
            for n in range(KT):
                act.dma_start(xT[:, n, :], xT_in[:, n, :]).then_inc(x_loaded[n], 16)
            act.dma_start(lbl[:], lb_logits).then_inc(lb_loaded, 16)
            act.sem_inc(unit_done, W_CREDIT)

            def split_hi(cst, it=0, width=None):
                if isinstance(it, int):
                    if cst + 4 * it > last:
                        return
                    width = WIDTH[cst + 4 * it]
                act.wait_ge(raw_loaded[cst % 2], 16 * (cst // 2 + 1) + 32 * it)
                act.wait_ge(unit_done, cst + 1 + 4 * it)
                A(w_hi[:, cst % 4, 0:width], raw[:, cst % 2, 0:width], ACT.Copy).then_inc(hi_done, 1)

            def x_tile(r, it, q, split):
                n = 2 * it + q
                a = 8 * r + n
                act.wait_ge(x_done, 8 * (r - 1) + n + 1 + BANK_CREDIT)
                act.wait_ge(sum_done, a)
                A(sq[:], xT[:, n, :], ACT.Square).then_inc(sq_done, 1)
                if split:
                    A(h_hi[:, n, :], xT[:, n, :], ACT.Copy,
                      scale=gain[:, bass.ds(8 * r + n, 1)]).then_inc(hh_done, 1)
                if r == 3:
                    act.wait_ge(sq_done, a + 1)
                    A(xT[:, n, :], xT[:, n, :], ACT.Copy,
                      scale=gain[:, bass.ds(8 * r + n, 1)]).then_inc(scaled, 1)

            def ffn(k):
                base, f0 = BASE[f"up{k}"], FT * (k - 1)

                def up_body(it, static):
                    for q in range(2):
                        f = f0 + 2 * it + q
                        split_hi(base + 2 * q + AHEAD, it, UW)
                        split_hi(base + 2 * q + 1 + AHEAD, it, UW)
                        act.wait_ge(gate_read, f + 1 + BANK_CREDIT)
                        A(sg[:], gn[:], ACT.Sigmoid).then_inc(sig_done, 1)
                        act.wait_ge(act_done, f + 1)
                        A(g_hi[:, 2 * it + q, :], un[:], ACT.Copy).then_inc(ghi_done, 1)

                with act.Fori(0, FT // 2 - 1) as it:
                    up_body(it, False)
                up_body(FT // 2 - 1, True)
                base, r = BASE[f"down{k}"], 1 if k == 1 else 3

                def down_body(it):
                    for q in range(2):
                        for w in range(2):
                            split_hi(base + 2 * q + w + AHEAD, it, DW)
                        x_tile(r, it, q, split=k == 1)

                with act.Fori(0, KT // 2 - 1) as it:
                    down_body(it)
                down_body(KT // 2 - 1)

            act.wait_ge(const_loaded, 16)
            for n in range(KT):
                act.wait_ge(x_loaded[n], 16)
                A(h_hi[:, n, :], xT[:, n, :], ACT.Copy, scale=gain[:, n:n + 1]).then_inc(hh_done, 1)
                if n in (0, 4):
                    split_hi(n // 4)
            for n in range(KT):
                if n:
                    act.wait_ge(sum_done, n)
                A(sq[:], xT[:, n, :], ACT.Square).then_inc(sq_done, 1)
                if n == 2:
                    split_hi(2)
            ffn(1)

            def prob_t_copy(q):
                act.wait_ge(pt_done, 2 * q + 1)
                if q:
                    act.wait_ge(pv_done, q)
                A(prob_t[:, 0, :, :].rearrange("p a b -> p (a b)"), ps[:, 4, :], ACT.Copy).then_inc(pta_done, 1)

            def exp_scores(q):
                for a in range(2):
                    act.wait_ge(nm_done, 2 * q + 1 + a)
                    if q:
                        act.wait_ge(pt_done, 2 * q - 1 + a)
                    A(prob[:, a, :], ps[:, 2 + a, :], ACT.Exp, bias=neg_max[:, q, a:a + 1],
                      accum_out=prob_sum[:, q, a:a + 1]).then_inc(p_done, 1)

            def y_hi(t):
                act.wait_ge(yt_done, 4 * t + 4)
                A(ya_hi[:, t, :], ps[:, 7, :], ACT.Copy).then_inc(yahi_done, 1)

            act.dma_start(consts[:], mix_const).then_inc(mix_loaded, 16)
            nc.scalar.preload_act_table_set("natural_log_exp_and_others")
            act.wait_ge(lb_ready, 1)
            A(lbt[:], lbt[:], ACT.Exp).then_inc(lb_exp, 1)
            base = BASE["proj"]
            for i, (kind, t) in enumerate(PROJ):
                for n in {0: (0, 1), 1: ()}.get(i, (i,)):
                    split_hi(base + n + AHEAD)
                if kind in ("ak", "aq"):
                    m = i - 1
                    act.wait_ge(proj_read, i + 1 + BANK_CREDIT)
                    if m:
                        act.wait_ge(qms_done, m)
                    A(q_sq[:], qk[:, m, :], ACT.Square).then_inc(qsq_done, 1)
                if 2 <= i <= 6:
                    m = i - 2
                    act.wait_ge(qeps_done, m + 1)
                    if m:
                        act.wait_ge(qn_done, m)
                    A(q_rs[:], q_ms[:], ACT.Ln).then_inc(act_seq, 1)
                    act.wait_ge(act_seq, m + 1)
                    A(q_rs[:], q_rs[:], ACT.Exp, scale=-0.5).then_inc(qr_done, 1)
                w = V_TILES.get(i - 1)
                if w is not None:
                    act.wait_ge(vt_done, w + 1)
                    vt = ps[:, 7, :].rearrange("p (a b) -> p a b", b=P)
                    A(v_a[:] if w == 0 else v_h[:, :, P * (w - 1):P * w], vt, ACT.Copy).then_inc(vn_done, 1)
                q = i - FIRST_ITEM
                if q >= 7 and q % 4 == 3:
                    y_hi(q // 4 - 1)
                if q >= 1:
                    prob_t_copy(q - 1)
                if q >= 0:
                    exp_scores(q)
            prob_t_copy(ITEMS - 1)
            y_hi(3)

            act.wait_ge(proj_read, len(PROJ) + BANK_CREDIT)
            for h in range(HH):
                A(forget[:, h, :], forget[:, h, :], ACT.Sigmoid).then_inc(fs_done, 1)
                dst = (o_ms, o_rs)[h % 2]
                if h >= 2:
                    act.wait_ge(sil_done, h - 1)
                else:
                    act.wait_ge(rope_done, 5)
                A(dst[:], (hq if h < 4 else hgate)[:, h % 4, :], ACT.Sigmoid).then_inc(sl_done, 1)

            nc.scalar.preload_act_table_set("natural_log_exp_and_others")

            def log_f(h):
                act.wait_ge(f_done, h + 1)
                act.wait_ge(k_done, h + 1)
                A(forget[:, h, :], forget[:, h, :], ACT.Ln).then_inc(lf_done, 1)

            def exponentials(h):
                act.wait_ge(d1_done, h + 1)
                if h:
                    act.wait_ge(sc_done, h)
                A(q_sc[:], k_sc[h % 2][:], ACT.Exp).then_inc(e1_done, 1)
                act.wait_ge(e1_done, h + 1)
                A(k_sc[h % 2][:], k_sc[h % 2][:], ACT.Exp, scale=-1.0).then_inc(e2_done, 1)
                act.wait_ge(d3_done, h + 1)
                A(k_end[:], k_end[:], ACT.Exp).then_inc(e3_done, 1)
                A(decay[:, h % 2, :], b_last[:], ACT.Exp)
                A(b_cum[h % 2][:], b_cum[h % 2][:], ACT.Exp).then_inc(e4_done, 1)

            log_f(0)
            exponentials(0)
            for h in range(HH):
                if h + 1 < HH:
                    log_f(h + 1)
                act.wait_ge(kt_done, h + 1)
                if h:
                    act.wait_ge(con_done, h)
                A(k_nat[:], ps[:, 6, :], ACT.Copy).then_inc(kn_done, 1)
                if h + 1 < HH:
                    exponentials(h + 1)
                if h % 2:
                    t = h // 2
                    act.wait_ge(ocopy_done, t + 1)
                    A(o_ms[:], o_t[:], ACT.Square).then_inc(osq_done, 1)
                    act.wait_ge(oeps_done, t + 1)
                    A(o_rs[:], o_ms[:], ACT.Ln).then_inc(act_seq, 1)
                    act.wait_ge(act_seq, 5 + t + 1)
                    A(o_rs[:], o_rs[:], ACT.Exp, scale=-0.5).then_inc(or_done, 1)
                    act.wait_ge(on_done, t + 1)
                    A(yb[:, 2 * t, :], o_u[:], ACT.Copy).then_inc(ybhi_done, 1)

            base = BASE["merge"]

            def merge_body(it):
                for q in range(4):
                    n = 4 * it + q
                    for w in range(3):
                        cst = base + 3 * q + w + AHEAD
                        if isinstance(it, int):
                            split_hi(cst + 12 * it)
                        else:
                            split_hi(cst, 3 * it, UW)
                        if w == 0:
                            act.wait_ge(ga_read, n + 1 + 1)
                            A(sga[:], sga[:], ACT.Sigmoid).then_inc(sga_done, 1)
                        if w == 1:
                            act.wait_ge(gb_read, n + 1 + 1)
                            A(sgb[:], sgb[:], ACT.Sigmoid).then_inc(sgb_done, 1)
                    act.wait_ge(m_done, n + 1)
                    A(m_hi[:, n, :], sga[:], ACT.Copy).then_inc(mhi_done, 1)

            with act.Fori(0, 2) as it:
                merge_body(it)
            base = BASE["wout"]

            def wout_body(it):
                for q in range(4):
                    n = 4 * it + q
                    split_hi(base + q + AHEAD, it, UW)
                    x_tile(2, 2 * it, q, True)

            with act.Fori(0, 2) as it:
                wout_body(it)
            ffn(2)

        @block.vector
        def _(dve):
            V = nc.vector
            seq = [0]

            def link(ins):
                seq[0] += 1
                ins.then_inc(dve_seq, 1)
                dve.wait_ge(dve_seq, seq[0])

            def tt(out, a, b, op):
                return V.tensor_tensor(out, a, b, op)

            def stt(out, a, s, b, op0, op1):
                return V.scalar_tensor_tensor(out, a, s, b, op0, op1)

            def split_lo(cst, it=0, width=None):
                if isinstance(it, int):
                    if cst + 4 * it > last:
                        return
                    width = WIDTH[cst + 4 * it]
                dve.wait_ge(hi_done, cst + 1 + 4 * it)
                tt(w_lo[:, cst % 4, 0:width], raw[:, cst % 2, 0:width], w_hi[:, cst % 4, 0:width].bitcast(F32),
                   ALU.subtract).then_inc(lo_done, 1)

            def newton(y, v, tmp):
                link(tt(tmp, y, y, ALU.mult))
                link(stt(tmp, tmp, -0.5, v, ALU.mult, ALU.mult))
                return stt(y, tmp, 1.5, y, ALU.add, ALU.mult)

            def rms_factor(m):
                dve.wait_ge(mean_done, m + 1)
                link(V.tensor_scalar(norm_v[:], ps[:, MEAN_BANK, 0:ST], 1.0 / D, EPS, ALU.mult, ALU.add))
                link(V.tensor_scalar(norm_y[:].bitcast(I32), norm_v[:].bitcast(I32), -0.5, float(0x5F3759DF), ALU.mult, ALU.add))
                for _ in range(3):
                    link(newton(norm_y[:], norm_v[:], norm_t[:]))
                tt(sq[:].rearrange("p (a b) -> p a b", b=P), ident.unsqueeze(1).to_broadcast([P, ST, P]),
                   norm_y[:].unsqueeze(2).to_broadcast([P, ST, P]), ALU.mult).then_inc(diag_done, 1)

            def rms_rows(m):
                dve.wait_ge(spread_done, m + 1)
                V.tensor_copy(rs[:], ps[:, MEAN_BANK, :]).then_inc(rs_done, 1)
                dve.wait_ge(rs_done, m + 1)

            def h_tile(r, it, q):
                n = 2 * it + q
                dve.wait_ge(hh_done, 8 * r + n + 1)
                stt(h_lo[:, n, :], xT[:, n, :], gain[:, bass.ds(8 * r + n, 1)], h_hi[:, n, :].bitcast(F32),
                    ALU.mult, ALU.subtract).then_inc(h_done, 1)

            def residual(r, it, q, done, factor):
                n = 2 * it + q
                dve.wait_ge(unit_done, done)
                stt(xT[:, n, :], ps[:, RES_BANKS + q % 2, :], factor, xT[:, n, :], ALU.mult, ALU.add).then_inc(x_done, 1)

            def ffn(k):
                base, f0 = BASE[f"up{k}"], FT * (k - 1)

                def up_body(it, first=False):
                    for q in range(2):
                        f = f0 + 2 * it + q
                        c0 = base + 2 * q
                        split_lo(c0 + AHEAD, it, UW)
                        if first and q == 0:
                            rms_factor(0 if k == 1 else 2)
                            split_lo(c0 + 1 + AHEAD, it, UW)
                            rms_rows(0 if k == 1 else 2)
                        dve.wait_ge(unit_done, c0 + 4 * it + 1 + W_CREDIT)
                        tt(gn[:], ps[:, UP_BANKS[0] + q, :], rs[:], ALU.mult).then_inc(gate_read, 1)
                        if not (first and q == 0):
                            split_lo(c0 + 1 + AHEAD, it, UW)
                        dve.wait_ge(unit_done, c0 + 1 + 4 * it + 1 + W_CREDIT)
                        tt(un[:], ps[:, UP_BANKS[1] + q, :], rs[:], ALU.mult).then_inc(up_read, 1)
                        dve.wait_ge(up_read, f + 1 + BANK_CREDIT)
                        tt(un[:], un[:], gn[:], ALU.mult).then_inc(prod_done, 1)
                        dve.wait_ge(prod_done, f + 1)
                        dve.wait_ge(sig_done, f + 1)
                        tt(un[:], un[:], sg[:], ALU.mult).then_inc(act_done, 1)
                        dve.wait_ge(ghi_done, f + 1)
                        tt(g_lo[:, 2 * it + q, :], un[:], g_hi[:, 2 * it + q, :].bitcast(F32), ALU.subtract).then_inc(glo_done, 1)
                        dve.wait_ge(glo_done, f + 1)

                up_body(0, True)
                with dve.Fori(1, FT // 2 - 1) as it:
                    up_body(it)
                up_body(FT // 2 - 1)
                base, r = BASE[f"down{k}"], 1 if k == 1 else 3

                def down_body(it):
                    for q in range(2):
                        for w in range(2):
                            split_lo(base + 2 * q + w + AHEAD, it, DW)
                        residual(r, it, q, base + 2 * q + 1 + 4 * it + 1 + W_CREDIT, 0.5)
                        if k == 1:
                            h_tile(r, it, q)

                with dve.Fori(0, KT // 2 - 1) as it:
                    down_body(it)
                down_body(KT // 2 - 1)

            dve.sem_inc(lo_done, RAW_CREDIT)
            for s in (gate_read, up_read, x_done, proj_read):
                dve.sem_inc(s, BANK_CREDIT)
            for s in (ga_read, gb_read, br_read):
                dve.sem_inc(s, 1)
            for n in range(KT):
                h_tile(0, 0, n)
                if n in (0, 4):
                    split_lo(n // 4)
            split_lo(2)
            ffn(1)

            def attention_step(q):
                if q >= 7 and q % 4 == 3:
                    t = q // 4 - 1
                    dve.wait_ge(yahi_done, t + 1)
                    tt(ya_lo[:, t, :], ps[:, 7, :], ya_hi[:, t, :].bitcast(F32), ALU.subtract).then_inc(yalo_done, 1)
                if 0 <= q - 2 < ITEMS:
                    dve.wait_ge(pv_done, q - 1)
                    link(V.reciprocal(inv_sum[:], prob_sum[:, q - 2, :]))
                    if q - 2 >= 2:
                        dve.wait_ge(yt_done, q - 3)
                    for a in range(2):
                        cols = slice(HD * a, HD * (a + 1))
                        ins = V.tensor_scalar(y_nat[:, q % 2, cols], ps[:, 6, cols], inv_sum[:, a:a + 1], None, ALU.mult)
                    ins.then_inc(yn_done, 1)
                if 0 <= q - 1 < ITEMS:
                    dve.wait_ge(pt_done, 2 * q)
                    V.tensor_copy(prob_t[:, 1, :, :].rearrange("p a b -> p (a b)"), ps[:, 5, :]).then_inc(ptb_done, 1)
                if 0 <= q < ITEMS:
                    for a in range(2):
                        dve.wait_ge(s_done, 2 * q + 1 + a)
                        V.reduce_max(neg_max[:, q, a:a + 1], ps[:, 2 + a, :], AX.X, negate=True).then_inc(nm_done, 1)

            dve.wait_ge(lb_loaded, 16)
            link(tt(lb[:], lbl[:, 0, :], lbl[:, 1, :], ALU.max))
            tt(lbt[:, 0, :], lbl[:, 0, :], lb[:], ALU.subtract)
            tt(lbt[:, 1, :], lbl[:, 1, :], lb[:], ALU.subtract).then_inc(lb_ready, 1)
            V.tensor_scalar(gq8[:], gain[:, 32:33], HD ** -0.5, None, ALU.mult)
            dve.wait_ge(lb_exp, 1)
            link(tt(lb[:], lbt[:, 0, :], lbt[:, 1, :], ALU.add))
            link(V.reciprocal(lb[:], lb[:]))
            link(tt(lb[:], lb[:], lbt[:, 0, :], ALU.mult))
            link(V.tensor_scalar(one_minus_lb[:], lb[:], -1.0, 1.0, ALU.mult, ALU.add))

            base = BASE["proj"]
            for i, (kind, t) in enumerate(PROJ):
                if i != 1:
                    split_lo(base + i + AHEAD)
                if i == 0:
                    rms_factor(1)
                    split_lo(base + 1 + AHEAD)
                    rms_rows(1)
                w = V_TILES.get(i)
                if w:
                    dve.wait_ge(vt_done, w)
                dst = {"av": v_tmp[:], "hi": v_tmp[:], "ak": qk[:, 0, :], "aq": qk[:, min(1 + t, 4), :], "hf": forget[:, t, :],
                       "hq": hq[:, t % 4, :], "hg": hgate[:, t % 4, :]}[kind]
                dve.wait_ge(unit_done, base + i + 1 + W_CREDIT)
                tt(dst, ps[:, i % 2, :], rs[:], ALU.mult).then_inc(proj_read, 1)
                if 3 <= i <= 7:
                    m = i - 3
                    dve.wait_ge(qr_done, m + 1)
                    link(newton(q_rs[:], q_ms[:], q_t[:]))
                    stt(qk[:, m, :], qk[:, m, :], gain[:, 33:34] if m == 0 else gq8[:], q_rs[:],
                        ALU.mult, ALU.mult).then_inc(qn_done, 1)
                if 2 <= i <= 6:
                    m = i - 2
                    dve.wait_ge(qms_done, m + 1)
                    if m:
                        dve.wait_ge(qn_done, m)
                    V.tensor_scalar(q_ms[:], ps[:, 4, :], EPS, None, ALU.add).then_inc(qeps_done, 1)
                if 5 <= i <= 9:
                    m = i - 5
                    dve.wait_ge(mix_loaded, 16)
                    dve.wait_ge(qswap_done, m + 1)
                    dve.wait_ge(qn_done, min(i - 2, 5))
                    tt(q_t[:], ps[:, 5, :], c["sin"], ALU.mult)
                    link(tt(qk[:, m, :], qk[:, m, :], c["cos"], ALU.mult))
                    tt(qk[:, m, :], qk[:, m, :], q_t[:], ALU.add).then_inc(rope_done, 1)
                    dve.wait_ge(rope_done, m + 1)
                attention_step(i - FIRST_ITEM)
            for q in range(ITEMS, ITEMS + 4):
                attention_step(q)

            for j in range(2 * 4):
                dve.wait_ge(sl_done, j + 1)
                dst = (hq if j < 4 else hgate)[:, j % 4, :]
                tt(dst, dst, (o_ms, o_rs)[j % 2][:], ALU.mult).then_inc(sil_done, 1)

            fwd, bwd = slice(0, HD), slice(HD, P)
            chunks = lambda t: t.rearrange("p (n c) -> p n c", c=CHUNK)

            def f_gate(h):
                dve.wait_ge(fs_done, h + 1)
                V.tensor_scalar(forget[:, h, :], forget[:, h, :], one_minus_lb[:, h:h + 1], lb[:, h:h + 1],
                                ALU.mult, ALU.add).then_inc(f_done, 1)

            def cumulate(h):
                b, par = b_cum[h % 2], h % 2
                dve.wait_ge(lf_done, h + 1)
                if h >= 2:
                    dve.wait_ge(o_done, h - 1)
                V.tensor_tensor_scan(b[fwd, :], c["keep"][fwd, :], forget[fwd, h, :], 0.0, ALU.mult, ALU.add)
                link(V.tensor_tensor_scan(b[bwd, ::-1], c["keep"][bwd, ::-1], forget[bwd, h, ::-1], 0.0, ALU.mult, ALU.add))
                if h:
                    dve.wait_ge(e4_done, h)
                b3 = chunks(b[:])
                V.tensor_copy(b_last[fwd, :], b3[fwd, :, CHUNK - 1])
                V.tensor_copy(b_last[bwd, :], b3[bwd, :, 0]).then_inc(bl_done, 1)
                V.tensor_copy(b_mid[fwd, :], b3[fwd, :, CHUNK // 2 - 1])
                link(V.tensor_copy(b_mid[bwd, :], b3[bwd, :, CHUNK // 2]))
                tt(chunks(k_sc[par][:]), b3, b_mid[:].unsqueeze(2).to_broadcast([P, NCH, CHUNK]), ALU.subtract).then_inc(d1_done, 1)

            def duplicate_q(h):
                src = hq[slice(HD * (h % 2), HD * (h % 2) + HD), h // 2, :]
                V.tensor_copy(q_dup[fwd, :], src)
                link(V.tensor_copy(q_dup[bwd, :], src))

            dve.wait_ge(zero_done, 2)
            f_gate(0)
            cumulate(0)
            dve.wait_ge(sil_done, 8)
            duplicate_q(0)
            for h in range(HH):
                par, t, r = h % 2, h // 2, h % 2
                if h + 1 < HH:
                    f_gate(h + 1)
                dve.wait_ge(e1_done, h + 1)
                tt(q_sc[:], q_sc[:], q_dup[:], ALU.mult).then_inc(qs_done, 1)
                dve.wait_ge(e2_done, h + 1)
                dve.wait_ge(ke_done, h + 1)
                tt(k_sc[par][:], k_sc[par][:], k_in[par][:], ALU.mult).then_inc(ks_done, 1)
                dve.wait_ge(e4_done, h + 1)
                tt(b_cum[par][:], b_cum[par][:], q_dup[:], ALU.mult).then_inc(qe_done, 1)
                if h + 1 < HH:
                    cumulate(h + 1)
                    dve.wait_ge(qe_done, h + 1)
                    duplicate_q(h + 1)
                if h:
                    dve.wait_ge(o_done, h)
                for d in range(2):
                    dve.wait_ge(sc_done, h + 1)
                    ins = V.copy_predicated(sc_m[:, d, :].rearrange("p (a b) -> p a b", b=P),
                                            c["mask"][:, P * d:P * (d + 1)].bitcast(U32).unsqueeze(1).to_broadcast([P, ST, P]),
                                            ps[:, 2 + d, :].rearrange("p (a b) -> p a b", b=P))
                ins.then_inc(scm_done, 1)
                dve.wait_ge(con_done, h + 1)
                con = ps[:, 4:6, :].rearrange("p a (n e) -> p (a n) e", e=HD)
                for j in range(NCH - 1):
                    nb = NCH - 1 - j
                    stt(state[fwd, j + 1, :], state[fwd, j, :], decay[fwd, par, j:j + 1], con[fwd, j, :], ALU.mult, ALU.add)
                    ins = stt(state[bwd, nb - 1, :], state[bwd, nb, :], decay[bwd, par, nb:nb + 1], con[bwd, nb, :], ALU.mult, ALU.add)
                    if j < NCH - 2:
                        link(ins)
                ins.then_inc(state_done, 1)
                if r:
                    dve.wait_ge(o_done, h + 1)
                    V.tensor_copy(o_t[:], ps[:, 7, :]).then_inc(ocopy_done, 1)
                    dve.wait_ge(oms_done, t + 1)
                    V.tensor_scalar(o_ms[:], ps[:, 6, :], EPS, None, ALU.add).then_inc(oeps_done, 1)
                    dve.wait_ge(or_done, t + 1)
                    link(newton(o_rs[:], o_ms[:], o_u[:]))
                    link(stt(o_t[:], o_t[:], gain[:, 34 + t:35 + t], o_rs[:], ALU.mult, ALU.mult))
                    tt(o_u[:], o_t[:], hgate[:, t, :], ALU.mult).then_inc(on_done, 1)
                    dve.wait_ge(ybhi_done, t + 1)
                    tt(yb[:, 2 * t + 1, :], o_u[:], yb[:, 2 * t, :].bitcast(F32), ALU.subtract).then_inc(yblo_done, 1)
                    dve.wait_ge(yblo_done, t + 1)

            base = BASE["merge"]

            def merge_body(it):
                for q in range(4):
                    n = 4 * it + q
                    for w in range(3):
                        cst = base + 3 * q + w
                        if isinstance(it, int):
                            split_lo(cst + AHEAD + 12 * it)
                        else:
                            split_lo(cst + AHEAD, 3 * it, UW)
                        dve.wait_ge(unit_done, cst + 12 * it + 1 + W_CREDIT)
                        if w == 0:
                            tt(sga[:], ps[:, 0, :], rs[:], ALU.mult).then_inc(ga_read, 1)
                        if w == 1:
                            tt(sgb[:], ps[:, 1, :], rs[:], ALU.mult).then_inc(gb_read, 1)
                    dve.wait_ge(sga_done, n + 1)
                    tt(sga[:], ps[:, 2, :], sga[:], ALU.mult)
                    dve.wait_ge(sgb_done, n + 1)
                    tt(sgb[:], ps[:, 3, :], sgb[:], ALU.mult).then_inc(br_read, 1)
                    dve.wait_ge(br_read, n + 1 + 1)
                    tt(sga[:], sga[:], sgb[:], ALU.add).then_inc(m_done, 1)
                    dve.wait_ge(mhi_done, n + 1)
                    tt(m_lo[:, n, :], sga[:], m_hi[:, n, :].bitcast(F32), ALU.subtract).then_inc(mlo_done, 1)
                    dve.wait_ge(mlo_done, n + 1)

            with dve.Fori(0, 2) as it:
                merge_body(it)
            base = BASE["wout"]

            def wout_body(it):
                for q in range(4):
                    split_lo(base + q + AHEAD, it, UW)
                    residual(2, 2 * it, q, base + q + 4 * it + 1 + W_CREDIT, 1.0)
                    h_tile(2, 2 * it, q)

            with dve.Fori(0, 2) as it:
                wout_body(it)
            ffn(2)
            rms_factor(3)
            rms_rows(3)
            for n in range(POOL_OUT[0]):
                dve.wait_ge(scaled, n + 1)
                tt(xT[:, n, :], xT[:, n, :], rs[:], ALU.mult).then_inc(out_dve, 1)

        @block.tensor
        def _(pe):
            T = nc.tensor

            def product(bank, slot, tiles, moving_hi, moving_lo, first_wait=None, start=True, stop=True, off=0):
                for j in range(tiles):
                    if first_wait:
                        first_wait(j)
                    cols = slice(P * (off + j), P * (off + j + 1))
                    T.matmul(ps[:, bank, :], w_hi[:, slot, cols], moving_hi(j), start=start and j == 0, stop=False)
                    T.matmul(ps[:, bank, :], w_hi[:, slot, cols], moving_lo(j), start=False, stop=False)
                    ins = T.matmul(ps[:, bank, :], w_lo[:, slot, cols], moving_hi(j), start=False,
                                   stop=stop and j == tiles - 1)
                return ins

            def h_unit(bank, cst, wait=None):
                return product(bank, cst % 4, KT, lambda j: h_hi[:, j, :], lambda j: h_lo[:, j, :], wait)

            def h_wait(m):
                return lambda j: pe.wait_ge(h_done, 8 * m + j + 1)

            def mean(m):
                pe.wait_ge(sum_done, 8 * m + 8)
                if m == 0:
                    pe.wait_ge(small_loaded, 16)
                for j in range(ST):
                    ins = T.matmul(ps[:, MEAN_BANK, j:j + 1], sq_sum[:, P * j:P * (j + 1)], ones[:, 0:1], start=True, stop=True)
                ins.then_inc(mean_done, 1)

            def spread(m):
                pe.wait_ge(diag_done, m + 1)
                T.matmul(ps[:, MEAN_BANK, :], ones, sq[:], start=True, stop=True).then_inc(spread_done, 1)

            def ffn(k):
                base, f0, m = BASE[f"up{k}"], FT * (k - 1), 2 * (k - 1)

                def up_body(it, first=False):
                    for q in range(2):
                        for w, read in ((0, gate_read), (1, up_read)):
                            cst = base + 2 * q + w
                            pe.wait_ge(lo_done, cst + 4 * it + 1 + RAW_CREDIT)
                            pe.wait_ge(read, f0 + 2 * it + q + 1)
                            wait = h_wait(m) if first and q == 0 and w == 0 else None
                            h_unit(UP_BANKS[w] + q, cst, wait).then_inc(unit_done, 1)
                            if first and 2 * q + w == (2 if m == 0 else 0):
                                mean(m)
                            if first and 2 * q + w == (3 if m == 0 else 1):
                                spread(m)

                up_body(0, True)
                with pe.Fori(1, FT // 2) as it:
                    up_body(it)
                base, r = BASE[f"down{k}"], 0 if k == 1 else 2

                def down_body(it, first=False):
                    for q in range(2):
                        pe.wait_ge(x_done, 8 * r + 2 * it + q + 1)
                        for w in range(2):
                            cst = base + 2 * q + w
                            pe.wait_ge(lo_done, cst + 4 * it + 1 + RAW_CREDIT)
                            wait = (lambda j: pe.wait_ge(glo_done, f0 + FT // 2 * w + j + 1)) if first and q == 0 else None
                            product(RES_BANKS + q, cst % 4, FT // 2, lambda j: g_hi[:, FT // 2 * w + j, :],
                                    lambda j: g_lo[:, FT // 2 * w + j, :], wait, start=w == 0, stop=w == 1).then_inc(unit_done, 1)

                down_body(0, True)
                with pe.Fori(1, KT // 2) as it:
                    down_body(it)

            ffn(1)

            base = BASE["proj"]

            def scores(q):
                t, qt = q // 4, q % 4
                if q == 0:
                    pe.wait_ge(rope_done, 5)
                for a in range(2):
                    if q:
                        pe.wait_ge(p_done, 2 * q - 1 + a)
                    rows = slice(HD * a, HD * (a + 1))
                    T.matmul(ps[:, 2 + a, :], qk[rows, 1 + t, P * qt:P * (qt + 1)], qk[rows, 0, :],
                             start=True, stop=True).then_inc(s_done, 1)

            def prob_transposes(q):
                for a, ev in ((0, pta_done), (1, ptb_done)):
                    pe.wait_ge(p_done, 2 * q + 1 + a)
                    if q:
                        pe.wait_ge(ev, q)
                    for j in range(ST):
                        ins = T.transpose(ps[:, 4 + a, P * j:P * (j + 1)], prob[:, a, P * j:P * (j + 1)], ident)
                    ins.then_inc(pt_done, 1)

            def weighted(q):
                if q:
                    pe.wait_ge(yn_done, q)
                pe.wait_ge(vn_done, 1)
                for a, ev in ((0, pta_done), (1, ptb_done)):
                    pe.wait_ge(ev, q + 1)
                    for j in range(ST):
                        ins = T.matmul(ps[:, 6, HD * a:HD * (a + 1)], prob_t[:, a, j, :], v_a[:, j, HD * a:HD * (a + 1)],
                                       start=j == 0, stop=j == ST - 1)
                ins.then_inc(pv_done, 1)

            def y_transpose(q):
                t, qt = q // 4, q % 4
                pe.wait_ge(yn_done, q + 1)
                if q == 0:
                    pe.wait_ge(vn_done, 5)
                if t and qt == 0:
                    pe.wait_ge(yalo_done, t)
                T.transpose(ps[:, 7, P * qt:P * (qt + 1)], y_nat[:, q % 2, :], ident).then_inc(yt_done, 1)

            def items(q):
                if 0 <= q - 3 < ITEMS:
                    y_transpose(q - 3)
                if 0 <= q - 2 < ITEMS:
                    weighted(q - 2)
                if 0 <= q - 1 < ITEMS:
                    prob_transposes(q - 1)
                if 0 <= q < ITEMS:
                    scores(q)

            for i, (kind, t) in enumerate(PROJ):
                cst = base + i
                pe.wait_ge(lo_done, cst + 1 + RAW_CREDIT)
                pe.wait_ge(proj_read, i + 1)
                h_unit(i % 2, cst, h_wait(1) if i == 0 else None).then_inc(unit_done, 1)
                if i == 0:
                    mean(1)
                    spread(1)
                    pe.wait_ge(mix_loaded, 16)
                w = V_TILES.get(i - 1)
                if w is not None:
                    pe.wait_ge(proj_read, i + BANK_CREDIT)
                    if w:
                        pe.wait_ge(vn_done, w)
                    for j in range(ST):
                        ins = T.transpose(ps[:, 7, P * j:P * (j + 1)], v_tmp[:, P * j:P * (j + 1)], ident)
                    ins.then_inc(vt_done, 1)
                if 2 <= i <= 6:
                    m = i - 2
                    pe.wait_ge(qsq_done, m + 1)
                    if m:
                        pe.wait_ge(qeps_done, m)
                    T.matmul(ps[:, 4, :], c["head_mean"], q_sq[:], start=True, stop=True).then_inc(qms_done, 1)
                if 4 <= i <= 8:
                    m = i - 4
                    pe.wait_ge(qn_done, m + 1)
                    if m:
                        pe.wait_ge(rope_done, m)
                    T.matmul(ps[:, 5, :], c["swap"], qk[:, m, :], start=True, stop=True).then_inc(qswap_done, 1)
                items(i - FIRST_ITEM)
            for q in range(ITEMS, ITEMS + 3):
                items(q)

            fwd, bwd = slice(0, HD), slice(HD, P)
            for h in range(HH):
                par, t, r = h % 2, h // 2, h % 2
                pe.wait_ge(ke_done, h + 1)
                if h and h % 2 == 0:
                    pe.wait_ge(oeps_done, t)
                if h:
                    pe.wait_ge(kn_done, h)
                for j in range(ST):
                    ins = T.transpose(ps[:, 6, P * j:P * (j + 1)], k_end[:, P * j:P * (j + 1)], ident)
                ins.then_inc(kt_done, 1)
                pe.wait_ge(qs_done, h + 1)
                pe.wait_ge(ks_done, h + 1)
                if h:
                    pe.wait_ge(scm_done, h)
                for d, rows in enumerate((fwd, bwd)):
                    for j in range(ST):
                        cols = slice(P * j, P * (j + 1))
                        ins = T.matmul(ps[:, 2 + d, cols], k_sc[par][rows, cols], q_sc[rows, cols], start=True, stop=True)
                ins.then_inc(sc_done, 1)
                pe.wait_ge(kn_done, h + 1)
                pe.wait_ge(vexp_done, h + 1)
                if h:
                    pe.wait_ge(state_done, h)
                for j in range(ST):
                    ins = T.matmul(ps[:, 4 + j // 2, 256 * (j % 2):256 * (j % 2 + 1)], k_nat[:, P * j:P * (j + 1)],
                                   v_exp[:, j, :, :].rearrange("p a b -> p (a b)"), start=True, stop=True)
                ins.then_inc(con_done, 1)
                pe.wait_ge(scm_done, h + 1)
                pe.wait_ge(qe_done, h + 1)
                pe.wait_ge(state_done, h + 1)
                if r == 0 and t:
                    pe.wait_ge(ocopy_done, t)
                rows = slice(HD * r, HD * (r + 1))
                for j in range(ST):
                    v_t = v_h[:, j, HD * h:HD * (h + 1)]
                    cols = slice(P * j, P * (j + 1))
                    for d in range(2):
                        T.matmul(ps[rows, 7, cols], v_t, sc_m[:, d, cols], start=d == 0, stop=False)
                    for n in range(4 * j, 4 * j + 4):
                        cc = slice(CHUNK * n, CHUNK * (n + 1))
                        ins = T.matmul(ps[rows, 7, cc], state[:, n, :], b_cum[par][:, cc], start=False, stop=n == 4 * j + 3)
                ins.then_inc(o_done, 1)
                if r:
                    pe.wait_ge(osq_done, t + 1)
                    T.matmul(ps[:, 6, :], c["head_mean"], o_ms[:], start=True, stop=True).then_inc(oms_done, 1)

            base = BASE["merge"]
            pe.wait_ge(yalo_done, 4)
            pe.wait_ge(yblo_done, PAIRS)

            def merge_body(it):
                for q in range(4):
                    n = 4 * it + q
                    for w in range(3):
                        cst = base + 3 * q + w
                        pe.wait_ge(lo_done, cst + 12 * it + 1 + RAW_CREDIT)
                        if w < 2:
                            pe.wait_ge((ga_read, gb_read)[w], n + 1)
                            h_unit(w, cst).then_inc(unit_done, 1)
                        else:
                            pe.wait_ge(br_read, n + 1)
                            product(2, cst % 4, 4, lambda j: ya_hi[:, j, :], lambda j: ya_lo[:, j, :])
                            product(3, cst % 4, 4, lambda j: yb[:, 2 * j, :], lambda j: yb[:, 2 * j + 1, :], off=4).then_inc(unit_done, 1)

            with pe.Fori(0, 2) as it:
                merge_body(it)
            base = BASE["wout"]

            def wout_body(it, first=False):
                for q in range(4):
                    cst = base + q
                    pe.wait_ge(lo_done, cst + 4 * it + 1 + RAW_CREDIT)
                    pe.wait_ge(x_done, 8 + 4 * it + q + 1)
                    wait = (lambda j: pe.wait_ge(mlo_done, j + 1)) if first and q == 0 else None
                    product(RES_BANKS + q % 2, cst % 4, KT, lambda j: m_hi[:, j, :], lambda j: m_lo[:, j, :], wait).then_inc(unit_done, 1)

            wout_body(0, True)
            wout_body(1)
            ffn(2)
            mean(3)
            spread(3)


def kernel(**inputs):
    import concourse.bacc as bacc
    from concourse.bass_utils import run_bass_kernel_spmd

    a = {k: np.asarray(v) for k, v in inputs.items()}

    def square_units(w, order):
        t = w.reshape(w.shape[0] // P, P, w.shape[1])
        return np.stack([np.ascontiguousarray(t[:, :, cols].transpose(1, 0, 2)).reshape(P, -1) for cols in order])

    def block(j):
        return np.arange(P * j, P * (j + 1))

    def up(k):
        gate = square_units(a[f"ffn{k}_w_gate"][0], [block(j) for j in range(FT)])
        upw = square_units(a[f"ffn{k}_w_up"][0], [block(j) for j in range(FT)])
        return np.stack([gate, upw], axis=1).reshape(2 * FT, P, UW)

    def down(k):
        w = square_units(a[f"ffn{k}_w_down"][0], [block(j) for j in range(KT)])
        return np.ascontiguousarray(w.reshape(KT, P, 2, DW).transpose(0, 2, 1, 3)).reshape(2 * KT, P, DW)

    at, start = {}, 0
    for name, width in (("aq", NH * HD), ("ak", P), ("av", P), ("hq", S), ("ff", S), ("fb", S), ("hi", S), ("hg", S),
                        ("ga", D), ("gb", D)):
        at[name] = start
        start += width
    head = np.arange(HD)

    def cols(kind, t):
        if kind == "aq":
            return at["aq"] + np.concatenate([HD * t + head, HD * (t + 4) + head])
        if kind == "hf":
            return np.concatenate([at["ff"] + HD * t + head, at["fb"] + HD * t + head])
        return at[kind] + block(t)

    w_in = a["w_in"][0]
    proj = square_units(w_in, [cols(kind, t) for kind, t in PROJ])
    pair_rows = np.concatenate([np.concatenate([HD * t + head, HD * (t + 4) + head]) for t in range(4)])
    branches = np.concatenate([a["w_branch_attn"][0][pair_rows], a["w_branch_hgrn"][0]], axis=0)
    branch = square_units(branches, [block(j) for j in range(KT)])
    gates = [square_units(w_in, [cols(g, j) for j in range(KT)]) for g in ("ga", "gb")]
    merge = np.stack([*gates, branch], axis=1).reshape(3 * KT, P, UW)
    wout = square_units(a["w_out"][0], [block(j) for j in range(KT)])

    def column_tiles(v):
        return v.reshape(-1, P).T

    gains = np.concatenate([column_tiles(a["ffn1_norm_g"][0]), column_tiles(a["mix_norm_g"][0]), column_tiles(a["ffn2_norm_g"][0]),
                            column_tiles(a["final_norm_g"]), np.concatenate([a["q_norm_g"][0]] * 2)[:, None],
                            np.concatenate([a["k_norm_g"][0]] * 2)[:, None], column_tiles(a["hgrn_out_norm_g"][0]),
                            (np.arange(P)[:, None] // CHUNK == np.arange(4)[None]).astype(np.float32)], axis=1)
    lb = a["hgrn_lb_logits"].reshape(2, 2, HH, HD).transpose(0, 3, 1, 2).reshape(P, 2, HH)

    grid_w, n_freq = 64, HD // 4
    inv = (np.float32(10000.0) ** (-np.arange(n_freq, dtype=np.float32) / np.float32(n_freq))).astype(np.float32)
    pos = np.arange(S)
    ang = np.concatenate([(pos // grid_w).astype(np.float32)[:, None] * inv, (pos % grid_w).astype(np.float32)[:, None] * inv], axis=1)
    p = np.arange(P)
    cos = np.cos(ang).astype(np.float32)[:, p % 32].T
    sin = np.sin(ang).astype(np.float32)[:, p % 32].T * np.where(p % HD < 32, -1.0, 1.0)[:, None]
    keep = np.where(p[:, None] < HD, pos[None] % CHUNK != 0, pos[None] % CHUNK != CHUNK - 1)
    same = p[:, None] // CHUNK == p[None] // CHUNK
    mask = np.concatenate([same & (p[:, None] <= p[None]), same & (p[:, None] >= p[None])], axis=1)
    swap = (p // HD * HD + (p % HD + 32) % HD)[:, None] == p[None]
    head_mean = (p[:, None] // HD == p[None] // HD) / HD
    consts = np.concatenate([cos, sin, keep, mask, head_mean, swap], axis=1).astype(np.float32)

    xT = a["x"][0].reshape(S, KT, P).transpose(2, 1, 0)
    arrays = {
        "xT": xT, "up1": up(1), "down1": down(1), "proj": proj, "merge": merge, "wout": wout, "up2": up(2), "down2": down(2),
        "mix_const": consts, "small_const": np.concatenate([np.ones((P, P)), np.eye(P)], axis=1).astype(np.float32), "gains": gains, "lb_logits": lb,
    }
    arrays = {k: np.ascontiguousarray(v) for k, v in arrays.items()}
    nc = bacc.Bacc("TRN2", target_bir_lowering=False, num_devices=1)
    args = [nc.dram_tensor(f"{k}_dram", v.shape, F32, kind="ExternalInput").ap() for k, v in arrays.items()]
    out = nc.dram_tensor("outT_dram", (P, KT, S), F32, kind="ExternalOutput").ap()
    build(nc, *args, out)
    got = run_bass_kernel_spmd(nc, [{f"{k}_dram": v for k, v in arrays.items()}], core_ids=[0]).results[0]["outT_dram"]
    return np.ascontiguousarray(np.asarray(got).transpose(2, 1, 0).reshape(1, S, D))
```

```python
from contextlib import ExitStack

import numpy as np

import concourse.bass as bass
from concourse import mybir

F32 = mybir.dt.float32
F32R = mybir.dt.float32r
I32 = mybir.dt.int32
U32 = mybir.dt.uint32
ALU = mybir.AluOpType
ACT = mybir.ActivationFunctionType
AX = mybir.AxisListType

P = 128
D, S, FF = 1024, 512, 2816
HD = 64
NH, NKV = 8, 2
HH = 8
CHUNK = 32
NCH = S // CHUNK
EPS = 1e-6
KT = D // P
FT = FF // P
ST = S // P
UW = KT * P
DW = FT // 2 * P
RAW_SLOTS, W_SLOTS, AHEAD = 2, 4, 3
PAIRS = HH // 2

STREAMS = [("up1", 2 * FT, UW), ("down1", 2 * KT, DW), ("proj", 26, UW), ("gates", 2 * KT, UW),
           ("branch", KT, UW),
           ("wout", KT, UW), ("up2", 2 * FT, UW), ("down2", 2 * KT, DW)]
BASE, WIDTH = {}, []
for _name, _count, _width in STREAMS:
    BASE[_name] = len(WIDTH)
    WIDTH += [_width] * _count
UNITS = len(WIDTH)

PROJ = ([("av", 0), ("ak", 0)] + [("aq", t) for t in range(4)] + [("hi", t) for t in range(4)]
        + [("hf", h) for h in range(HH)] + [("hq", t) for t in range(4)] + [("hg", t) for t in range(4)])
V_TILES = {i: w for w, i in enumerate(i for i, (kind, _) in enumerate(PROJ) if kind in ("av", "hi"))}
FIRST_ITEM = 9

GATES_ATTN, GATES_SILU, GATES_HEAD = [0, 1], [2, 3], [[4, 5], [6], [7], [8], [9], [10], [11, 12], [13]]
GATE_PLACES = ([("x", n) for n in range(6)] + [("hq", 0), ("hq", 1), ("hgate", 0), ("hq", 2), ("hgate", 1), ("hq", 3),
               ("k_in0", 0), ("hgate", 2), ("v_exp", 0), ("v_exp", 1)])
GATES_LAST = [14, 15]
GONE = -1e5
ITEMS = 4 * ST

MIX_CONSTS = [("cos", S), ("sin", S), ("keep", S), ("mask", 2 * P), ("head_mean", P), ("swap", P)]
MIX_COLS = sum(w for _, w in MIX_CONSTS)


def build(nc, xT_in, up1, down1, proj, gates, branch, wout, up2, down2, mix_const, small_const, gains, lb_logits, x_spill, outT):
    with ExitStack() as ctx:
        def sb(name, shape, dt=F32):
            return ctx.enter_context(nc.sbuf_tensor(name, shape, dt))

        def sem(name):
            return ctx.enter_context(nc.semaphore(name))

        xT = sb("xT", [P, KT, S])
        h_hi, h_lo = sb("h_hi", [P, KT, S], F32R), sb("h_lo", [P, KT, S], F32R)
        raw = sb("raw", [P, RAW_SLOTS, DW])
        w_hi, w_lo = sb("w_hi", [P, W_SLOTS, DW], F32R), sb("w_lo", [P, W_SLOTS, DW], F32R)
        rs = sb("rs", [P, S])
        sq_sum = sb("sq_sum", [P, S])
        sq = sb("sq", [P, S])
        small = sb("small", [P, 2 * P])
        ones, ident = small[:, 0:P], small[:, P:2 * P]
        norm_v, norm_y, norm_t = (sb(n, [P, ST]) for n in ("norm_v", "norm_y", "norm_t"))
        gain = sb("gain", [P, 42])
        gq8 = sb("gq8", [P, 1])
        lbl = sb("lbl", [P, 2, HH])
        lb, one_minus_lb = sb("lb", [P, HH]), sb("one_minus_lb", [P, HH])
        lbt = sb("lbt", [P, 2, HH])
        neg_max, prob_sum = sb("neg_max", [P, ITEMS, 2]), sb("prob_sum", [P, ITEMS, 2])
        inv_sum = sb("inv_sum", [P, 2])
        b_mid = sb("b_mid", [P, NCH])
        b_last = sb("b_last", [P, NCH + 2])

        REGION = 96 * 1024
        region_at = -(-nc.sbuf_base // 32) * 32
        sb("region", [P, REGION // 4 + 8])
        ffn_words = 2 * FT * S

        def at(name, kib, shape, dt=F32):
            n = 4 * int(np.prod(shape[1:]))
            assert kib * 1024 + n <= REGION, name
            return nc.alloc_sbuf_tensor_at(name, shape, dt, offset=region_at + int(kib * 1024))

        assert ffn_words * 4 <= 88 * 1024
        g_hi, g_lo = at("g_hi", 0, [P, FT, S], F32R), at("g_lo", 44, [P, FT, S], F32R)
        gn, sg, un = at("gn", 88, [P, S]), at("sg", 90, [P, S]), at("un", 92, [P, S])

        forget = at("forget", 0, [P, HH, S])
        yb = at("yb", 0, [P, 2 * PAIRS, S], F32R)
        ya_hi, ya_lo = at("ya_hi", 16, [P, 4, S], F32R), at("ya_lo", 24, [P, 4, S], F32R)
        hq, hgate = at("hq", 32, [P, 4, S]), at("hgate", 40, [P, 4, S])
        v_h = at("v_h", 48, [P, ST, S])
        consts = at("consts", 56, [P, MIX_COLS])
        c = {}
        col = 0
        for name, width in MIX_CONSTS:
            c[name] = consts[:, col:col + width]
            col += width
        qk = at("qk", 64, [P, 5, S])
        v_a = at("v_a", 74, [P, ST, P])
        prob = at("prob", 76, [P, 2, S])
        prob_t = at("prob_t", 80, [P, 2, ST, P])
        y_nat = at("y_nat", 84, [P, 2, P])
        v_tmp = at("v_tmp", 85, [P, S])
        q_sq, q_ms, q_rs, q_t = (at(n, 87 + 2 * i, [P, S]) for i, n in enumerate(("q_sq", "q_ms", "q_rs", "q_t")))
        k_in = [at("k_in0", 64, [P, S]), sq_sum]
        b_cum = [at("b_cum0", 66, [P, S]), at("b_cum1", 68, [P, S])]
        k_sc = [at("k_sc0", 70, [P, S]), at("k_sc1", 72, [P, S])]
        q_sc, k_end, q_dup = at("q_sc", 74, [P, S]), at("k_end", 76, [P, S]), at("q_dup", 78, [P, S])
        k_nat = sq
        sc_m = at("sc_m", 80, [P, 2, S])
        state = at("state", 84, [P, HD, NCH])
        decay = xT[:, 6:8, :].rearrange("p a b -> p (a b)")
        v_exp = at("v_exp", 88, [P, ST, HD, 4])
        o_ms, o_rs = at("o_ms", 92, [P, S]), at("o_rs", 94, [P, S])
        o_t = at("o_t", 56, [P, S])
        o_u = at("o_u", 58, [P, S])
        m_hi, m_lo = at("m_hi", 66, [P, KT, S], F32R), at("m_lo", 48, [P, KT, S], F32R)
        halves = v_exp[:].rearrange("p (i a) e c -> p i (a e c)", i=2)
        places = {"x": xT, "hq": hq, "hgate": hgate, "v_exp": halves, "k_in0": k_in[0][:].unsqueeze(1)}
        gate_at = [places[name][:, n, :] for name, n in GATE_PLACES]

        ps = ctx.enter_context(nc.psum_tensor("ps", [P, 8, S], F32))
        UP_BANKS, RES_BANKS, MEAN_BANK = (0, 2), 4, 6

        raw_loaded = [sem(f"raw_loaded{i}") for i in range(RAW_SLOTS)]
        x_loaded = [sem(f"x_loaded{n}") for n in range(KT)]
        const_loaded, small_loaded, mix_loaded = sem("const_loaded"), sem("small_loaded"), sem("mix_loaded")
        hi_done, lo_done, unit_done = sem("hi_done"), sem("lo_done"), sem("unit_done")
        x_done, sq_done, sum_done = sem("x_done"), sem("sq_done"), sem("sum_done")
        hh_done, h_done, mean_done = sem("hh_done"), sem("h_done"), sem("mean_done")
        diag_done, spread_done, rs_done = sem("diag_done"), sem("spread_done"), sem("rs_done")
        gate_read, up_read, sig_done = sem("gate_read"), sem("up_read"), sem("sig_done")
        prod_done, act_done, ghi_done, glo_done = sem("prod_done"), sem("act_done"), sem("ghi_done"), sem("glo_done")
        dve_seq, act_seq, pool_seq = sem("dve_seq"), sem("act_seq"), sem("pool_seq")
        lb_loaded, lb_exp, lb_ready = sem("lb_loaded"), sem("lb_exp"), sem("lb_ready")
        proj_read = sem("proj_read")
        vt_done, vn_done = sem("vt_done"), sem("vn_done")
        qsq_done, qms_done, qeps_done, qr_done = sem("qsq_done"), sem("qms_done"), sem("qeps_done"), sem("qr_done")
        qn_done, qswap_done, rope_done = sem("qn_done"), sem("qswap_done"), sem("rope_done")
        s_done, nm_done, p_done, pt_done = sem("s_done"), sem("nm_done"), sem("p_done"), sem("pt_done")
        pta_done, ptb_done, pv_done, yn_done = sem("pta_done"), sem("ptb_done"), sem("pv_done"), sem("yn_done")
        yt_done, yahi_done, yalo_done = sem("yt_done"), sem("yahi_done"), sem("yalo_done")
        fs_done, sl_done, sil_done = sem("fs_done"), sem("sl_done"), sem("sil_done")
        f_done, k_done, lf_done, b_done = sem("f_done"), sem("k_done"), sem("lf_done"), sem("b_done")
        d1_done, d3_done, bl_done = sem("d1_done"), sem("d3_done"), sem("bl_done")
        e5_done = sem("e5_done")
        e1_done, e2_done, e3_done, e4_done = sem("e1_done"), sem("e2_done"), sem("e3_done"), sem("e4_done")
        qs_done, ks_done, ke_done, qe_done = sem("qs_done"), sem("ks_done"), sem("ke_done"), sem("qe_done")
        sc_done, scm_done, kt_done, kn_done = sem("sc_done"), sem("scm_done"), sem("kt_done"), sem("kn_done")
        zero_done, vexp_done, con_done, state_done = sem("zero_done"), sem("vexp_done"), sem("con_done"), sem("state_done")
        o_done, ocopy_done, osq_done, oms_done = sem("o_done"), sem("ocopy_done"), sem("osq_done"), sem("oms_done")
        oeps_done, or_done, on_done, ybhi_done, yblo_done = (sem(n) for n in (
            "oeps_done", "or_done", "on_done", "ybhi_done", "yblo_done"))
        spilled, x_back, sgate_done = sem("spilled"), sem("x_back"), sem("sgate_done")
        br_read, m_done, mhi_done, mlo_done = sem("br_read"), sem("m_done"), sem("mhi_done"), sem("mlo_done")
        scaled, out_dve, out_pool, out_stored = sem("scaled"), sem("out_dve"), sem("out_pool"), sem("out_stored")
        POOL_OUT = (5, 6, 7)
        RAW_CREDIT, W_CREDIT, BANK_CREDIT = RAW_SLOTS, W_SLOTS, 2

        block = ctx.enter_context(nc.Block())
        last = UNITS - 1

        @block.sync
        def _(sp):
            for name, count, width in STREAMS:
                src, base = dict(up1=up1, down1=down1, proj=proj, gates=gates, branch=branch, wout=wout, up2=up2, down2=down2)[name], BASE[name]
                with sp.Fori(0, count // 2) as it:
                    for i in range(2):
                        sp.wait_ge(lo_done, 2 * it + base + i + 1)
                        sp.dma_start(raw[:, i, 0:width], src[2 * it + i, :, :]).then_inc(raw_loaded[i], 16)
            for n in (0, 1, 5, 2, 3, 6, 4, 7):
                if n in POOL_OUT:
                    sp.wait_ge(out_pool, n - POOL_OUT[0] + 1)
                else:
                    sp.wait_ge(out_dve, n + 1)
                sp.dma_start(outT[:, n, :], xT[:, n, :]).then_inc(out_stored, 16)
            sp.wait_ge(out_stored, 16 * KT)

        @block.gpsimd
        def _(pool):
            def accumulate(first, n_of, a):
                pool.wait_ge(sq_done, a + 1)
                if first:
                    nc.gpsimd.tensor_copy(sq_sum[:], sq[:]).then_inc(sum_done, 1)
                else:
                    pool.wait_ge(sum_done, a)
                    nc.gpsimd.tensor_tensor(sq_sum[:], sq_sum[:], sq[:], ALU.add).then_inc(sum_done, 1)

            for r in range(2):
                if r:
                    pool.wait_ge(mean_done, r)
                for n in range(KT):
                    accumulate(n == 0, n, 8 * r + n)
            pool.wait_ge(yalo_done, 4)
            pool.wait_ge(pv_done, ITEMS)
            nc.gpsimd.memset(sc_m[:], 0.0).then_inc(zero_done, 1)
            nc.gpsimd.memset(state[:], 0.0).then_inc(zero_done, 1)
            nc.gpsimd.memset(b_last[:], GONE).then_inc(zero_done, 1)
            pool.wait_ge(zero_done, 3)
            pool.wait_ge(vn_done, 5)

            def key(h):
                pool.wait_ge(f_done, h + 1)
                if h >= 2:
                    pool.wait_ge(ks_done, h - 1)
                nc.gpsimd.tensor_scalar(k_in[h % 2][:], forget[:, h, :], -1.0, 1.0, ALU.mult, ALU.add).then_inc(k_done, 1)

            def to_end(h):
                pool.wait_ge(bl_done, h + 1)
                if h >= 1:
                    pool.wait_ge(kt_done, h)
                chunks = lambda t: t[:].rearrange("p (n c) -> p n c", c=CHUNK)
                nc.gpsimd.tensor_tensor(chunks(k_end), b_last[:, 1:NCH + 1].unsqueeze(2).to_broadcast([P, NCH, CHUNK]), chunks(b_cum[h % 2]),
                                        ALU.subtract).then_inc(d3_done, 1)

            def key_to_end(h):
                pool.wait_ge(e3_done, h + 1)
                nc.gpsimd.tensor_tensor(k_end[:], k_end[:], k_in[h % 2][:], ALU.mult).then_inc(ke_done, 1)

            def value(h):
                if h >= 1:
                    pool.wait_ge(con_done, h)
                for j in range(4):
                    ins = nc.gpsimd.tensor_scalar(v_exp[:, :, :, j], v_h[:, :, HD * h:HD * (h + 1)], gain[:, 38 + j:39 + j], None, ALU.mult)
                ins.then_inc(vexp_done, 1)

            key(0)
            to_end(0)
            key(1)
            key_to_end(0)
            value(0)
            for h in range(HH - 1):
                to_end(h + 1)
                if h + 2 < HH:
                    key(h + 2)
                key_to_end(h + 1)
                value(h + 1)
            for r in range(2, 4):
                pool.wait_ge(mean_done, r)
                for n in range(KT):
                    accumulate(n == 0, n, 8 * r + n)
            for i, n in enumerate(POOL_OUT):
                pool.wait_ge(rs_done, 4)
                pool.wait_ge(scaled, n + 1)
                nc.gpsimd.tensor_tensor(xT[:, n, :], xT[:, n, :], rs[:], ALU.mult).then_inc(out_pool, 1)

        @block.scalar
        def _(act):
            A = nc.scalar.activation
            act.dma_start(gain[:], gains).then_inc(const_loaded, 16)
            act.dma_start(small[:], small_const).then_inc(small_loaded, 16)
            for n in range(KT):
                act.dma_start(xT[:, n, :], xT_in[:, n, :]).then_inc(x_loaded[n], 16)
            act.dma_start(lbl[:], lb_logits).then_inc(lb_loaded, 16)
            act.sem_inc(unit_done, W_CREDIT)

            def split_hi(cst, it=0, width=None):
                if isinstance(it, int):
                    if cst + 4 * it > last:
                        return
                    width = WIDTH[cst + 4 * it]
                act.wait_ge(raw_loaded[cst % 2], 16 * (cst // 2 + 1) + 32 * it)
                act.wait_ge(unit_done, cst + 1 + 4 * it)
                A(w_hi[:, cst % 4, 0:width], raw[:, cst % 2, 0:width], ACT.Copy).then_inc(hi_done, 1)

            def x_tile(r, it, q, split):
                n = 2 * it + q
                a = 8 * r + n
                act.wait_ge(x_done, 8 * (r - 1) + n + 1 + BANK_CREDIT)
                act.wait_ge(sum_done, a)
                A(sq[:], xT[:, n, :], ACT.Square).then_inc(sq_done, 1)
                if split:
                    A(h_hi[:, n, :], xT[:, n, :], ACT.Copy,
                      scale=gain[:, bass.ds(8 * r + n, 1)]).then_inc(hh_done, 1)
                if r == 3:
                    act.wait_ge(sq_done, a + 1)
                    A(xT[:, n, :], xT[:, n, :], ACT.Copy,
                      scale=gain[:, bass.ds(8 * r + n, 1)]).then_inc(scaled, 1)

            def ffn(k):
                base, f0 = BASE[f"up{k}"], FT * (k - 1)

                def up_body(it, static):
                    for q in range(2):
                        f = f0 + 2 * it + q
                        split_hi(base + 2 * q + AHEAD, it, UW)
                        split_hi(base + 2 * q + 1 + AHEAD, it, UW)
                        act.wait_ge(gate_read, f + 1 + BANK_CREDIT)
                        A(sg[:], gn[:], ACT.Sigmoid).then_inc(sig_done, 1)
                        act.wait_ge(act_done, f + 1)
                        A(g_hi[:, 2 * it + q, :], un[:], ACT.Copy).then_inc(ghi_done, 1)

                with act.Fori(0, FT // 2 - 1) as it:
                    up_body(it, False)
                up_body(FT // 2 - 1, True)
                base, r = BASE[f"down{k}"], 1 if k == 1 else 3

                def down_body(it):
                    for q in range(2):
                        for w in range(2):
                            split_hi(base + 2 * q + w + AHEAD, it, DW)
                        x_tile(r, it, q, split=k == 1)

                with act.Fori(0, KT // 2 - 1) as it:
                    down_body(it)
                down_body(KT // 2 - 1)

            act.wait_ge(const_loaded, 16)
            for n in range(KT):
                act.wait_ge(x_loaded[n], 16)
                A(h_hi[:, n, :], xT[:, n, :], ACT.Copy, scale=gain[:, n:n + 1]).then_inc(hh_done, 1)
                if n in (0, 4):
                    split_hi(n // 4)
            for n in range(KT):
                if n:
                    act.wait_ge(sum_done, n)
                A(sq[:], xT[:, n, :], ACT.Square).then_inc(sq_done, 1)
                if n == 2:
                    split_hi(2)
            ffn(1)

            def prob_t_copy(q):
                act.wait_ge(pt_done, 2 * q + 1)
                if q:
                    act.wait_ge(pv_done, q)
                A(prob_t[:, 0, :, :].rearrange("p a b -> p (a b)"), ps[:, 4, :], ACT.Copy).then_inc(pta_done, 1)

            def exp_scores(q):
                for a in range(2):
                    act.wait_ge(nm_done, 2 * q + 1 + a)
                    if q:
                        act.wait_ge(pt_done, 2 * q - 1 + a)
                    A(prob[:, a, :], ps[:, 2 + a, :], ACT.Exp, bias=neg_max[:, q, a:a + 1],
                      accum_out=prob_sum[:, q, a:a + 1]).then_inc(p_done, 1)

            def y_hi(t):
                act.wait_ge(yt_done, 4 * t + 4)
                A(ya_hi[:, t, :], ps[:, 7, :], ACT.Copy).then_inc(yahi_done, 1)

            act.dma_start(consts[:], mix_const).then_inc(mix_loaded, 16)
            act.wait_ge(h_done, 16)
            act.dma_start(x_spill, xT[:]).then_inc(spilled, 16)
            nc.scalar.preload_act_table_set("natural_log_exp_and_others")
            act.wait_ge(lb_ready, 1)
            A(lbt[:], lbt[:], ACT.Exp).then_inc(lb_exp, 1)
            base = BASE["proj"]
            for i, (kind, t) in enumerate(PROJ):
                for n in {0: (0, 1), 1: ()}.get(i, (i,)):
                    split_hi(base + n + AHEAD)
                if 3 <= i <= 7:
                    m = i - 3
                    act.wait_ge(qeps_done, m + 1)
                    if m:
                        act.wait_ge(qn_done, m)
                    A(q_rs[:], q_ms[:], ACT.Ln).then_inc(act_seq, 1)
                    act.wait_ge(act_seq, m + 1)
                    A(q_rs[:], q_rs[:], ACT.Exp, scale=-0.5).then_inc(qr_done, 1)
                if kind in ("ak", "aq"):
                    m = i - 1
                    act.wait_ge(proj_read, i + 1 + BANK_CREDIT)
                    if m:
                        act.wait_ge(qms_done, m)
                    A(q_sq[:], qk[:, m, :], ACT.Square).then_inc(qsq_done, 1)
                w = V_TILES.get(i - 1)
                if w is not None:
                    act.wait_ge(vt_done, w + 1)
                    vt = ps[:, 7, :].rearrange("p (a b) -> p a b", b=P)
                    A(v_a[:] if w == 0 else v_h[:, :, P * (w - 1):P * w], vt, ACT.Copy).then_inc(vn_done, 1)
                q = i - FIRST_ITEM
                if q >= 7 and q % 4 == 3:
                    y_hi(q // 4 - 1)
                if q >= 1:
                    prob_t_copy(q - 1)
                if 0 <= q < ITEMS:
                    exp_scores(q)
            gate_base = BASE["gates"]
            for g in GATES_ATTN:
                split_hi(gate_base + g + AHEAD)
            y_hi(3)
            for g in GATES_SILU:
                split_hi(gate_base + g + AHEAD)

            act.wait_ge(proj_read, len(PROJ) + BANK_CREDIT)
            for h in range(HH):
                A(forget[:, h, :], forget[:, h, :], ACT.Sigmoid).then_inc(fs_done, 1)
                dst = (o_ms, o_rs)[h % 2]
                if h >= 2:
                    act.wait_ge(sil_done, h - 1)
                else:
                    act.wait_ge(rope_done, 5)
                A(dst[:], (hq if h < 4 else hgate)[:, h % 4, :], ACT.Sigmoid).then_inc(sl_done, 1)

            nc.scalar.preload_act_table_set("natural_log_exp_and_others")

            def log_f(h):
                act.wait_ge(f_done, h + 1)
                act.wait_ge(k_done, h + 1)
                A(forget[:, h, :], forget[:, h, :], ACT.Ln).then_inc(lf_done, 1)

            def exponentials(h):
                act.wait_ge(d1_done, h + 1)
                if h:
                    act.wait_ge(sc_done, h)
                A(q_sc[:], k_sc[h % 2][:], ACT.Exp).then_inc(e1_done, 1)
                act.wait_ge(e1_done, h + 1)
                A(k_sc[h % 2][:], k_sc[h % 2][:], ACT.Exp, scale=-1.0).then_inc(e2_done, 1)
                act.wait_ge(d3_done, h + 1)
                A(k_end[:], k_end[:], ACT.Exp).then_inc(e3_done, 1)
                A(b_cum[h % 2][:], b_cum[h % 2][:], ACT.Exp).then_inc(e4_done, 1)

            def decays(h):
                if h:
                    act.wait_ge(state_done, h)
                else:
                    act.wait_ge(bl_done, 1)
                for rows, first in ((slice(0, HD), 0), (slice(HD, P), 2)):
                    ins = A(decay[rows, :].rearrange("p (e n) -> p e n", n=NCH),
                            b_last[rows, first:first + NCH].unsqueeze(1).to_broadcast([HD, HD, NCH]), ACT.Exp)
                ins.then_inc(e5_done, 1)

            def norm_exp(t):
                act.wait_ge(oeps_done, t + 1)
                A(o_rs[:], o_ms[:], ACT.Ln).then_inc(act_seq, 1)
                act.wait_ge(act_seq, 5 + t + 1)
                A(o_rs[:], o_rs[:], ACT.Exp, scale=-0.5).then_inc(or_done, 1)
                act.wait_ge(on_done, t + 1)
                A(yb[:, 2 * t, :], o_u[:], ACT.Copy).then_inc(ybhi_done, 1)

            def keys_to_sbuf(h):
                act.wait_ge(kt_done, h + 1)
                if h:
                    act.wait_ge(con_done, h)
                A(k_nat[:], ps[:, 6, :], ACT.Copy).then_inc(kn_done, 1)

            log_f(0)
            exponentials(0)
            log_f(1)
            act.wait_ge(spilled, 16)
            decays(0)
            keys_to_sbuf(0)
            for h in range(HH):
                for g in GATES_HEAD[h][:1]:
                    split_hi(gate_base + g + AHEAD)
                if h + 1 < HH:
                    exponentials(h + 1)
                if h + 2 < HH:
                    log_f(h + 2)
                for g in GATES_HEAD[h][1:]:
                    split_hi(gate_base + g + AHEAD)
                if h + 1 < HH:
                    decays(h + 1)
                    keys_to_sbuf(h + 1)
                if h and h % 2 == 0:
                    norm_exp(h // 2 - 1)
                if h % 2:
                    act.wait_ge(ocopy_done, h // 2 + 1)
                    A(o_ms[:], o_t[:], ACT.Square).then_inc(osq_done, 1)
            for g in GATES_LAST:
                split_hi(gate_base + g + AHEAD)
            norm_exp(PAIRS - 1)

            base = BASE["branch"]
            for n in range(KT):
                split_hi(base + n + AHEAD)
                for g in (2 * n, 2 * n + 1):
                    if g == 0:
                        act.wait_ge(proj_read, len(PROJ) + 2 * KT + BANK_CREDIT)
                    A(gate_at[g], gate_at[g], ACT.Sigmoid).then_inc(sgate_done, 1)
                act.wait_ge(m_done, n + 1)
                A(m_hi[:, n, :], gate_at[2 * n], ACT.Copy).then_inc(mhi_done, 1)
                if n == 4:
                    act.wait_ge(mlo_done, 4)
                    act.wait_ge(spilled, 16)
                    act.dma_start(xT[:], x_spill).then_inc(x_back, 16)
            base = BASE["wout"]

            def wout_body(it):
                for q in range(4):
                    n = 4 * it + q
                    split_hi(base + q + AHEAD, it, UW)
                    x_tile(2, 2 * it, q, True)

            with act.Fori(0, 2) as it:
                wout_body(it)
            ffn(2)

        @block.vector
        def _(dve):
            V = nc.vector
            seq = [0]

            def link(ins):
                seq[0] += 1
                ins.then_inc(dve_seq, 1)
                dve.wait_ge(dve_seq, seq[0])

            def tt(out, a, b, op):
                return V.tensor_tensor(out, a, b, op)

            def stt(out, a, s, b, op0, op1):
                return V.scalar_tensor_tensor(out, a, s, b, op0, op1)

            def split_lo(cst, it=0, width=None):
                if isinstance(it, int):
                    if cst + 4 * it > last:
                        return
                    width = WIDTH[cst + 4 * it]
                dve.wait_ge(hi_done, cst + 1 + 4 * it)
                tt(w_lo[:, cst % 4, 0:width], raw[:, cst % 2, 0:width], w_hi[:, cst % 4, 0:width].bitcast(F32),
                   ALU.subtract).then_inc(lo_done, 1)

            def newton(y, v, tmp):
                link(tt(tmp, y, y, ALU.mult))
                link(stt(tmp, tmp, -0.5, v, ALU.mult, ALU.mult))
                return stt(y, tmp, 1.5, y, ALU.add, ALU.mult)

            def rms_factor(m):
                dve.wait_ge(mean_done, m + 1)
                link(V.tensor_scalar(norm_v[:], ps[:, MEAN_BANK, 0:ST], 1.0 / D, EPS, ALU.mult, ALU.add))
                link(V.tensor_scalar(norm_y[:].bitcast(I32), norm_v[:].bitcast(I32), -0.5, float(0x5F3759DF), ALU.mult, ALU.add))
                for _ in range(3):
                    link(newton(norm_y[:], norm_v[:], norm_t[:]))
                tt(sq[:].rearrange("p (a b) -> p a b", b=P), ident.unsqueeze(1).to_broadcast([P, ST, P]),
                   norm_y[:].unsqueeze(2).to_broadcast([P, ST, P]), ALU.mult).then_inc(diag_done, 1)

            def rms_rows(m):
                dve.wait_ge(spread_done, m + 1)
                V.tensor_copy(rs[:], ps[:, MEAN_BANK, :]).then_inc(rs_done, 1)
                dve.wait_ge(rs_done, m + 1)

            def h_tile(r, it, q):
                n = 2 * it + q
                dve.wait_ge(hh_done, 8 * r + n + 1)
                stt(h_lo[:, n, :], xT[:, n, :], gain[:, bass.ds(8 * r + n, 1)], h_hi[:, n, :].bitcast(F32),
                    ALU.mult, ALU.subtract).then_inc(h_done, 1)

            def residual(r, it, q, done, factor):
                n = 2 * it + q
                dve.wait_ge(unit_done, done)
                stt(xT[:, n, :], ps[:, RES_BANKS + q % 2, :], factor, xT[:, n, :], ALU.mult, ALU.add).then_inc(x_done, 1)

            def ffn(k):
                base, f0 = BASE[f"up{k}"], FT * (k - 1)

                def up_body(it, first=False):
                    for q in range(2):
                        f = f0 + 2 * it + q
                        c0 = base + 2 * q
                        split_lo(c0 + AHEAD, it, UW)
                        if first and q == 0:
                            rms_factor(0 if k == 1 else 2)
                            split_lo(c0 + 1 + AHEAD, it, UW)
                            rms_rows(0 if k == 1 else 2)
                        dve.wait_ge(unit_done, c0 + 4 * it + 1 + W_CREDIT)
                        tt(gn[:], ps[:, UP_BANKS[0] + q, :], rs[:], ALU.mult).then_inc(gate_read, 1)
                        if not (first and q == 0):
                            split_lo(c0 + 1 + AHEAD, it, UW)
                        dve.wait_ge(unit_done, c0 + 1 + 4 * it + 1 + W_CREDIT)
                        tt(un[:], ps[:, UP_BANKS[1] + q, :], rs[:], ALU.mult).then_inc(up_read, 1)
                        dve.wait_ge(up_read, f + 1 + BANK_CREDIT)
                        tt(un[:], un[:], gn[:], ALU.mult).then_inc(prod_done, 1)
                        dve.wait_ge(prod_done, f + 1)
                        dve.wait_ge(sig_done, f + 1)
                        tt(un[:], un[:], sg[:], ALU.mult).then_inc(act_done, 1)
                        dve.wait_ge(ghi_done, f + 1)
                        tt(g_lo[:, 2 * it + q, :], un[:], g_hi[:, 2 * it + q, :].bitcast(F32), ALU.subtract).then_inc(glo_done, 1)
                        dve.wait_ge(glo_done, f + 1)

                up_body(0, True)
                with dve.Fori(1, FT // 2 - 1) as it:
                    up_body(it)
                up_body(FT // 2 - 1)
                base, r = BASE[f"down{k}"], 1 if k == 1 else 3

                def down_body(it):
                    for q in range(2):
                        for w in range(2):
                            split_lo(base + 2 * q + w + AHEAD, it, DW)
                        residual(r, it, q, base + 2 * q + 1 + 4 * it + 1 + W_CREDIT, 0.5)
                        if k == 1:
                            h_tile(r, it, q)

                with dve.Fori(0, KT // 2 - 1) as it:
                    down_body(it)
                down_body(KT // 2 - 1)

            dve.sem_inc(lo_done, RAW_CREDIT)
            for s in (gate_read, up_read, x_done, proj_read, br_read):
                dve.sem_inc(s, BANK_CREDIT)
            for n in range(KT):
                h_tile(0, 0, n)
                if n in (0, 4):
                    split_lo(n // 4)
            split_lo(2)
            ffn(1)

            def attention_step(q):
                if q >= 7 and q % 4 == 3:
                    t = q // 4 - 1
                    dve.wait_ge(yahi_done, t + 1)
                    tt(ya_lo[:, t, :], ps[:, 7, :], ya_hi[:, t, :].bitcast(F32), ALU.subtract).then_inc(yalo_done, 1)
                if 0 <= q - 2 < ITEMS:
                    dve.wait_ge(pv_done, q - 1)
                    link(V.reciprocal(inv_sum[:], prob_sum[:, q - 2, :]))
                    if q - 2 >= 2:
                        dve.wait_ge(yt_done, q - 3)
                    for a in range(2):
                        cols = slice(HD * a, HD * (a + 1))
                        ins = V.tensor_scalar(y_nat[:, q % 2, cols], ps[:, 6, cols], inv_sum[:, a:a + 1], None, ALU.mult)
                    ins.then_inc(yn_done, 1)
                if 0 <= q - 1 < ITEMS:
                    dve.wait_ge(pt_done, 2 * q)
                    V.tensor_copy(prob_t[:, 1, :, :].rearrange("p a b -> p (a b)"), ps[:, 5, :]).then_inc(ptb_done, 1)
                if 0 <= q < ITEMS:
                    for a in range(2):
                        dve.wait_ge(s_done, 2 * q + 1 + a)
                        V.reduce_max(neg_max[:, q, a:a + 1], ps[:, 2 + a, :], AX.X, negate=True).then_inc(nm_done, 1)

            dve.wait_ge(lb_loaded, 16)
            link(tt(lb[:], lbl[:, 0, :], lbl[:, 1, :], ALU.max))
            tt(lbt[:, 0, :], lbl[:, 0, :], lb[:], ALU.subtract)
            tt(lbt[:, 1, :], lbl[:, 1, :], lb[:], ALU.subtract).then_inc(lb_ready, 1)
            V.tensor_scalar(gq8[:], gain[:, 32:33], HD ** -0.5, None, ALU.mult)
            dve.wait_ge(lb_exp, 1)
            link(tt(lb[:], lbt[:, 0, :], lbt[:, 1, :], ALU.add))
            link(V.reciprocal(lb[:], lb[:]))
            link(tt(lb[:], lb[:], lbt[:, 0, :], ALU.mult))
            link(V.tensor_scalar(one_minus_lb[:], lb[:], -1.0, 1.0, ALU.mult, ALU.add))

            base = BASE["proj"]
            for i, (kind, t) in enumerate(PROJ):
                if i != 1:
                    split_lo(base + i + AHEAD)
                if i == 0:
                    rms_factor(1)
                    split_lo(base + 1 + AHEAD)
                    rms_rows(1)
                if 3 <= i <= 7:
                    m = i - 3
                    dve.wait_ge(qr_done, m + 1)
                    link(newton(q_rs[:], q_ms[:], q_t[:]))
                    stt(qk[:, m, :], qk[:, m, :], gain[:, 33:34] if m == 0 else gq8[:], q_rs[:],
                        ALU.mult, ALU.mult).then_inc(qn_done, 1)
                    dve.wait_ge(qn_done, m + 1)
                if 4 <= i <= 8:
                    m = i - 4
                    dve.wait_ge(mix_loaded, 16)
                    dve.wait_ge(qswap_done, m + 1)
                    tt(q_t[:], ps[:, 5, :], c["sin"], ALU.mult)
                    link(tt(qk[:, m, :], qk[:, m, :], c["cos"], ALU.mult))
                    tt(qk[:, m, :], qk[:, m, :], q_t[:], ALU.add).then_inc(rope_done, 1)
                    dve.wait_ge(rope_done, m + 1)
                w = V_TILES.get(i)
                if w:
                    dve.wait_ge(vt_done, w)
                dst = {"av": v_tmp[:], "hi": v_tmp[:], "ak": qk[:, 0, :], "aq": qk[:, min(1 + t, 4), :], "hf": forget[:, t, :],
                       "hq": hq[:, t % 4, :], "hg": hgate[:, t % 4, :]}[kind]
                dve.wait_ge(unit_done, base + i + 1 + W_CREDIT)
                tt(dst, ps[:, i % 2, :], rs[:], ALU.mult).then_inc(proj_read, 1)
                if 2 <= i <= 6:
                    m = i - 2
                    dve.wait_ge(qms_done, m + 1)
                    V.tensor_scalar(q_ms[:], ps[:, 4, :], EPS, None, ALU.add).then_inc(qeps_done, 1)
                attention_step(i - FIRST_ITEM)
            gate_base = BASE["gates"]

            def gate_lo(g):
                split_lo(gate_base + g + AHEAD)

            def gate_evac(g):
                if g == 0:
                    dve.wait_ge(spilled, 16)
                dve.wait_ge(unit_done, gate_base + g + 1 + W_CREDIT)
                tt(gate_at[g], ps[:, g % 2, :], rs[:], ALU.mult).then_inc(proj_read, 1)

            for q, g in zip(range(len(PROJ) - FIRST_ITEM, ITEMS + 3), GATES_ATTN):
                gate_lo(g)
                gate_evac(g)
                attention_step(q)
            attention_step(ITEMS + 3)
            for g in GATES_SILU:
                gate_lo(g)
                gate_evac(g)

            for j in range(2 * 4):
                dve.wait_ge(sl_done, j + 1)
                dst = (hq if j < 4 else hgate)[:, j % 4, :]
                tt(dst, dst, (o_ms, o_rs)[j % 2][:], ALU.mult).then_inc(sil_done, 1)

            fwd, bwd = slice(0, HD), slice(HD, P)
            chunks = lambda t: t.rearrange("p (n c) -> p n c", c=CHUNK)

            def f_gate(h):
                dve.wait_ge(fs_done, h + 1)
                V.tensor_scalar(forget[:, h, :], forget[:, h, :], one_minus_lb[:, h:h + 1], lb[:, h:h + 1],
                                ALU.mult, ALU.add).then_inc(f_done, 1)

            def cumulate(h):
                b, par = b_cum[h % 2], h % 2
                dve.wait_ge(lf_done, h + 1)
                if h >= 2:
                    dve.wait_ge(o_done, h - 1)
                V.tensor_tensor_scan(b[fwd, :], c["keep"][fwd, :], forget[fwd, h, :], 0.0, ALU.mult, ALU.add)
                link(V.tensor_tensor_scan(b[bwd, ::-1], c["keep"][bwd, ::-1], forget[bwd, h, ::-1], 0.0, ALU.mult, ALU.add))
                if h:
                    dve.wait_ge(e5_done, h)
                    dve.wait_ge(d3_done, h)
                b3 = chunks(b[:])
                V.tensor_copy(b_last[fwd, 1:NCH], b3[fwd, 0:NCH - 1, CHUNK - 1])
                V.tensor_copy(b_last[bwd, 2:NCH + 1], b3[bwd, 1:NCH, 0]).then_inc(bl_done, 1)
                V.tensor_copy(b_mid[fwd, :], b3[fwd, :, CHUNK // 2 - 1])
                link(V.tensor_copy(b_mid[bwd, :], b3[bwd, :, CHUNK // 2]))
                tt(chunks(k_sc[par][:]), b3, b_mid[:].unsqueeze(2).to_broadcast([P, NCH, CHUNK]), ALU.subtract).then_inc(d1_done, 1)

            def duplicate_q(h):
                src = hq[slice(HD * (h % 2), HD * (h % 2) + HD), h // 2, :]
                V.tensor_copy(q_dup[fwd, :], src)
                link(V.tensor_copy(q_dup[bwd, :], src))

            def mean_square(t):
                dve.wait_ge(oms_done, t + 1)
                V.tensor_scalar(o_ms[:], ps[:, 6, :], EPS, None, ALU.add).then_inc(oeps_done, 1)

            def normalize(t):
                dve.wait_ge(or_done, t + 1)
                link(newton(o_rs[:], o_ms[:], o_u[:]))
                link(stt(o_t[:], o_t[:], gain[:, 34 + t:35 + t], o_rs[:], ALU.mult, ALU.mult))
                tt(o_u[:], o_t[:], hgate[:, t, :], ALU.mult).then_inc(on_done, 1)
                dve.wait_ge(ybhi_done, t + 1)
                tt(yb[:, 2 * t + 1, :], o_u[:], yb[:, 2 * t, :].bitcast(F32), ALU.subtract).then_inc(yblo_done, 1)
                dve.wait_ge(yblo_done, t + 1)

            dve.wait_ge(zero_done, 3)
            def query_key(h):
                par = h % 2
                dve.wait_ge(e1_done, h + 1)
                tt(q_sc[:], q_sc[:], q_dup[:], ALU.mult).then_inc(qs_done, 1)
                dve.wait_ge(e2_done, h + 1)
                tt(k_sc[par][:], k_sc[par][:], k_in[par][:], ALU.mult).then_inc(ks_done, 1)
                dve.wait_ge(e4_done, h + 1)
                tt(b_cum[par][:], b_cum[par][:], q_dup[:], ALU.mult).then_inc(qe_done, 1)

            f_gate(0)
            cumulate(0)
            f_gate(1)
            dve.wait_ge(sil_done, 8)
            duplicate_q(0)
            query_key(0)
            for h in range(HH):
                par, t, r = h % 2, h // 2, h % 2
                for g in GATES_HEAD[h][:1]:
                    gate_lo(g)
                if h + 1 < HH:
                    cumulate(h + 1)
                    dve.wait_ge(qe_done, h + 1)
                    duplicate_q(h + 1)
                if h + 2 < HH:
                    f_gate(h + 2)
                if h:
                    dve.wait_ge(o_done, h)
                for d in range(2):
                    dve.wait_ge(sc_done, h + 1)
                    ins = V.copy_predicated(sc_m[:, d, :].rearrange("p (a b) -> p a b", b=P),
                                            c["mask"][:, P * d:P * (d + 1)].bitcast(U32).unsqueeze(1).to_broadcast([P, ST, P]),
                                            ps[:, 2 + d, :].rearrange("p (a b) -> p a b", b=P))
                ins.then_inc(scm_done, 1)
                for g in GATES_HEAD[h][:1]:
                    gate_evac(g)
                if h + 1 < HH:
                    query_key(h + 1)
                dve.wait_ge(con_done, h + 1)
                dve.wait_ge(e5_done, h + 1)
                con, flat, end = ps[:, 4:6, :].rearrange("p a b -> p (a b)"), state[:].rearrange("p e n -> p (e n)"), HD * NCH
                V.tensor_tensor_scan(flat[fwd, 1:end], decay[fwd, 1:end], con[fwd, 0:end - 1], 0.0, ALU.mult, ALU.add)
                V.tensor_tensor_scan(flat[bwd, 0:end - 1][:, ::-1], decay[bwd, 0:end - 1][:, ::-1], con[bwd, 1:end][:, ::-1], 0.0,
                                     ALU.mult, ALU.add).then_inc(state_done, 1)
                if r == 0 and t:
                    mean_square(t - 1)
                for g in GATES_HEAD[h][1:]:
                    gate_lo(g)
                    gate_evac(g)
                if r == 0 and t:
                    normalize(t - 1)
                if r:
                    dve.wait_ge(o_done, h + 1)
                    V.tensor_copy(o_t[:], ps[:, 7, :]).then_inc(ocopy_done, 1)
            for g in GATES_LAST:
                gate_lo(g)
                gate_evac(g)
            mean_square(PAIRS - 1)
            normalize(PAIRS - 1)

            base = BASE["branch"]
            for n in range(KT):
                ga, gb, bank = gate_at[2 * n], gate_at[2 * n + 1], 2 * (n % 2)
                split_lo(base + n + AHEAD)
                dve.wait_ge(unit_done, base + n + 1 + W_CREDIT)
                dve.wait_ge(sgate_done, 2 * n + 2)
                tt(ga, ps[:, bank, :], ga, ALU.mult)
                tt(gb, ps[:, bank + 1, :], gb, ALU.mult).then_inc(br_read, 1)
                dve.wait_ge(br_read, n + 1 + BANK_CREDIT)
                tt(ga, ga, gb, ALU.add).then_inc(m_done, 1)
                dve.wait_ge(mhi_done, n + 1)
                tt(m_lo[:, n, :], ga, m_hi[:, n, :].bitcast(F32), ALU.subtract).then_inc(mlo_done, 1)
            base = BASE["wout"]

            def wout_body(it):
                for q in range(4):
                    split_lo(base + q + AHEAD, it, UW)
                    residual(2, 2 * it, q, base + q + 4 * it + 1 + W_CREDIT, 1.0)
                    h_tile(2, 2 * it, q)

            dve.wait_ge(x_back, 16)
            with dve.Fori(0, 2) as it:
                wout_body(it)
            ffn(2)
            rms_factor(3)
            rms_rows(3)
            for n in range(POOL_OUT[0]):
                dve.wait_ge(scaled, n + 1)
                tt(xT[:, n, :], xT[:, n, :], rs[:], ALU.mult).then_inc(out_dve, 1)

        @block.tensor
        def _(pe):
            T = nc.tensor

            def product(bank, slot, tiles, moving_hi, moving_lo, first_wait=None, start=True, stop=True, off=0):
                for j in range(tiles):
                    if first_wait:
                        first_wait(j)
                    cols = slice(P * (off + j), P * (off + j + 1))
                    T.matmul(ps[:, bank, :], w_hi[:, slot, cols], moving_hi(j), start=start and j == 0, stop=False)
                    T.matmul(ps[:, bank, :], w_hi[:, slot, cols], moving_lo(j), start=False, stop=False)
                    ins = T.matmul(ps[:, bank, :], w_lo[:, slot, cols], moving_hi(j), start=False,
                                   stop=stop and j == tiles - 1)
                return ins

            def h_unit(bank, cst, wait=None):
                return product(bank, cst % 4, KT, lambda j: h_hi[:, j, :], lambda j: h_lo[:, j, :], wait)

            def h_wait(m):
                return lambda j: pe.wait_ge(h_done, 8 * m + j + 1)

            def mean(m):
                pe.wait_ge(sum_done, 8 * m + 8)
                if m == 0:
                    pe.wait_ge(small_loaded, 16)
                for j in range(ST):
                    ins = T.matmul(ps[:, MEAN_BANK, j:j + 1], sq_sum[:, P * j:P * (j + 1)], ones[:, 0:1], start=True, stop=True)
                ins.then_inc(mean_done, 1)

            def spread(m):
                pe.wait_ge(diag_done, m + 1)
                T.matmul(ps[:, MEAN_BANK, :], ones, sq[:], start=True, stop=True).then_inc(spread_done, 1)

            def ffn(k):
                base, f0, m = BASE[f"up{k}"], FT * (k - 1), 2 * (k - 1)

                def up_body(it, first=False):
                    for q in range(2):
                        for w, read in ((0, gate_read), (1, up_read)):
                            cst = base + 2 * q + w
                            pe.wait_ge(lo_done, cst + 4 * it + 1 + RAW_CREDIT)
                            pe.wait_ge(read, f0 + 2 * it + q + 1)
                            wait = h_wait(m) if first and q == 0 and w == 0 else None
                            h_unit(UP_BANKS[w] + q, cst, wait).then_inc(unit_done, 1)
                            if first and 2 * q + w == (2 if m == 0 else 0):
                                mean(m)
                            if first and 2 * q + w == (3 if m == 0 else 1):
                                spread(m)

                up_body(0, True)
                with pe.Fori(1, FT // 2) as it:
                    up_body(it)
                base, r = BASE[f"down{k}"], 0 if k == 1 else 2

                def down_body(it, first=False):
                    for q in range(2):
                        pe.wait_ge(x_done, 8 * r + 2 * it + q + 1)
                        for w in range(2):
                            cst = base + 2 * q + w
                            pe.wait_ge(lo_done, cst + 4 * it + 1 + RAW_CREDIT)
                            wait = (lambda j: pe.wait_ge(glo_done, f0 + FT // 2 * w + j + 1)) if first and q == 0 else None
                            product(RES_BANKS + q, cst % 4, FT // 2, lambda j: g_hi[:, FT // 2 * w + j, :],
                                    lambda j: g_lo[:, FT // 2 * w + j, :], wait, start=w == 0, stop=w == 1).then_inc(unit_done, 1)

                down_body(0, True)
                with pe.Fori(1, KT // 2) as it:
                    down_body(it)

            ffn(1)

            base = BASE["proj"]

            def scores(q):
                t, qt = q // 4, q % 4
                if q == 0:
                    pe.wait_ge(rope_done, 5)
                for a in range(2):
                    if q:
                        pe.wait_ge(p_done, 2 * q - 1 + a)
                    rows = slice(HD * a, HD * (a + 1))
                    T.matmul(ps[:, 2 + a, :], qk[rows, 1 + t, P * qt:P * (qt + 1)], qk[rows, 0, :],
                             start=True, stop=True).then_inc(s_done, 1)

            def prob_transposes(q):
                for a, ev in ((0, pta_done), (1, ptb_done)):
                    pe.wait_ge(p_done, 2 * q + 1 + a)
                    if q:
                        pe.wait_ge(ev, q)
                    for j in range(ST):
                        ins = T.transpose(ps[:, 4 + a, P * j:P * (j + 1)], prob[:, a, P * j:P * (j + 1)], ident)
                    ins.then_inc(pt_done, 1)

            def weighted(q):
                if q:
                    pe.wait_ge(yn_done, q)
                pe.wait_ge(vn_done, 1)
                for a, ev in ((0, pta_done), (1, ptb_done)):
                    pe.wait_ge(ev, q + 1)
                    for j in range(ST):
                        ins = T.matmul(ps[:, 6, HD * a:HD * (a + 1)], prob_t[:, a, j, :], v_a[:, j, HD * a:HD * (a + 1)],
                                       start=j == 0, stop=j == ST - 1)
                ins.then_inc(pv_done, 1)

            def y_transpose(q):
                t, qt = q // 4, q % 4
                pe.wait_ge(yn_done, q + 1)
                if q == 0:
                    pe.wait_ge(vn_done, 5)
                if t and qt == 0:
                    pe.wait_ge(yalo_done, t)
                T.transpose(ps[:, 7, P * qt:P * (qt + 1)], y_nat[:, q % 2, :], ident).then_inc(yt_done, 1)

            def items(q):
                if 0 <= q - 3 < ITEMS:
                    y_transpose(q - 3)
                if 0 <= q - 2 < ITEMS:
                    weighted(q - 2)
                if 0 <= q - 1 < ITEMS:
                    prob_transposes(q - 1)
                if 0 <= q < ITEMS:
                    scores(q)

            for i, (kind, t) in enumerate(PROJ):
                cst = base + i
                pe.wait_ge(lo_done, cst + 1 + RAW_CREDIT)
                pe.wait_ge(proj_read, i + 1)
                h_unit(i % 2, cst, h_wait(1) if i == 0 else None).then_inc(unit_done, 1)
                if i == 0:
                    mean(1)
                if i == 1:
                    spread(1)
                    pe.wait_ge(mix_loaded, 16)
                w = V_TILES.get(i - 1)
                if w is not None:
                    pe.wait_ge(proj_read, i + BANK_CREDIT)
                    if w:
                        pe.wait_ge(vn_done, w)
                    for j in range(ST):
                        ins = T.transpose(ps[:, 7, P * j:P * (j + 1)], v_tmp[:, P * j:P * (j + 1)], ident)
                    ins.then_inc(vt_done, 1)
                if 2 <= i <= 6:
                    m = i - 2
                    pe.wait_ge(qsq_done, m + 1)
                    if m:
                        pe.wait_ge(qeps_done, m)
                    T.matmul(ps[:, 4, :], c["head_mean"], q_sq[:], start=True, stop=True).then_inc(qms_done, 1)
                if 3 <= i <= 7:
                    m = i - 3
                    pe.wait_ge(qn_done, m + 1)
                    if m:
                        pe.wait_ge(rope_done, m)
                    T.matmul(ps[:, 5, :], c["swap"], qk[:, m, :], start=True, stop=True).then_inc(qswap_done, 1)
                items(i - FIRST_ITEM)
            def gate_unit(g):
                cst = BASE["gates"] + g
                pe.wait_ge(lo_done, cst + 1 + RAW_CREDIT)
                pe.wait_ge(proj_read, len(PROJ) + g + 1)
                h_unit(g % 2, cst).then_inc(unit_done, 1)

            for q, g in zip(range(len(PROJ) - FIRST_ITEM, ITEMS + 3), GATES_ATTN):
                gate_unit(g)
                items(q)
            for g in GATES_SILU:
                gate_unit(g)

            fwd, bwd = slice(0, HD), slice(HD, P)

            def mean_square(t):
                pe.wait_ge(osq_done, t + 1)
                T.matmul(ps[:, 6, :], c["head_mean"], o_ms[:], start=True, stop=True).then_inc(oms_done, 1)

            def key_transposes(h):
                pe.wait_ge(ke_done, h + 1)
                if h >= 3 and h % 2:
                    pe.wait_ge(oeps_done, h // 2)
                if h:
                    pe.wait_ge(kn_done, h)
                for j in range(ST):
                    ins = T.transpose(ps[:, 6, P * j:P * (j + 1)], k_end[:, P * j:P * (j + 1)], ident)
                ins.then_inc(kt_done, 1)

            def chunk_scores(h):
                pe.wait_ge(qs_done, h + 1)
                pe.wait_ge(ks_done, h + 1)
                if h:
                    pe.wait_ge(scm_done, h)
                for d, rows in enumerate((fwd, bwd)):
                    for j in range(ST):
                        cols = slice(P * j, P * (j + 1))
                        ins = T.matmul(ps[:, 2 + d, cols], k_sc[h % 2][rows, cols], q_sc[rows, cols], start=True, stop=True)
                ins.then_inc(sc_done, 1)

            def contributions(h):
                pe.wait_ge(kn_done, h + 1)
                pe.wait_ge(vexp_done, h + 1)
                if h:
                    pe.wait_ge(state_done, h)
                for j in range(ST):
                    for half in range(2):
                        ins = T.matmul(ps[:, 4 + half, :].rearrange("p (e n) -> p e n", n=NCH)[:, :, 4 * j:4 * j + 4],
                                       k_nat[:, P * j:P * (j + 1)], v_exp[:, j, HD // 2 * half:HD // 2 * (half + 1), :],
                                       start=True, stop=True)
                ins.then_inc(con_done, 1)

            def outputs(h):
                pe.wait_ge(scm_done, h + 1)
                pe.wait_ge(qe_done, h + 1)
                pe.wait_ge(state_done, h + 1)
                if h % 2 == 0 and h:
                    pe.wait_ge(ocopy_done, h // 2)
                rows = slice(HD * (h % 2), HD * (h % 2 + 1))
                for j in range(ST):
                    v_t = v_h[:, j, HD * h:HD * (h + 1)]
                    cols = slice(P * j, P * (j + 1))
                    for d in range(2):
                        T.matmul(ps[rows, 7, cols], v_t, sc_m[:, d, cols], start=d == 0, stop=False)
                    for n in range(4 * j, 4 * j + 4):
                        cc = slice(CHUNK * n, CHUNK * (n + 1))
                        ins = T.matmul(ps[rows, 7, cc], state[:, :, n], b_cum[h % 2][:, cc], start=False, stop=n == 4 * j + 3)
                ins.then_inc(o_done, 1)

            key_transposes(0)
            chunk_scores(0)
            for h in range(HH):
                for g in GATES_HEAD[h][:1]:
                    gate_unit(g)
                contributions(h)
                if h and h % 2 == 0:
                    mean_square(h // 2 - 1)
                for g in GATES_HEAD[h][1:]:
                    gate_unit(g)
                if h + 1 < HH:
                    key_transposes(h + 1)
                    chunk_scores(h + 1)
                outputs(h)
            for g in GATES_LAST:
                gate_unit(g)
            mean_square(PAIRS - 1)

            base = BASE["branch"]
            pe.wait_ge(yalo_done, 4)
            pe.wait_ge(yblo_done, PAIRS)
            pe.wait_ge(proj_read, len(PROJ) + 2 * KT + BANK_CREDIT)
            for n in range(KT):
                bank = 2 * (n % 2)
                pe.wait_ge(lo_done, base + n + 1 + RAW_CREDIT)
                pe.wait_ge(br_read, n + 1)
                slot = (base + n) % 4
                product(bank, slot, 4, lambda j: ya_hi[:, j, :], lambda j: ya_lo[:, j, :])
                product(bank + 1, slot, 4, lambda j: yb[:, 2 * j, :], lambda j: yb[:, 2 * j + 1, :], off=4).then_inc(unit_done, 1)
            base = BASE["wout"]

            def wout_body(it, first=False):
                for q in range(4):
                    cst = base + q
                    pe.wait_ge(lo_done, cst + 4 * it + 1 + RAW_CREDIT)
                    pe.wait_ge(x_done, 8 + 4 * it + q + 1)
                    wait = (lambda j: pe.wait_ge(mlo_done, j + 1)) if first and q == 0 else None
                    product(RES_BANKS + q % 2, cst % 4, KT, lambda j: m_hi[:, j, :], lambda j: m_lo[:, j, :], wait).then_inc(unit_done, 1)

            wout_body(0, True)
            wout_body(1)
            ffn(2)
            mean(3)
            spread(3)


def kernel(**inputs):
    import concourse.bacc as bacc
    from concourse.bass_utils import run_bass_kernel_spmd

    a = {k: np.asarray(v) for k, v in inputs.items()}

    def square_units(w, order):
        t = w.reshape(w.shape[0] // P, P, w.shape[1])
        return np.stack([np.ascontiguousarray(t[:, :, cols].transpose(1, 0, 2)).reshape(P, -1) for cols in order])

    def block(j):
        return np.arange(P * j, P * (j + 1))

    def up(k):
        gate = square_units(a[f"ffn{k}_w_gate"][0], [block(j) for j in range(FT)])
        upw = square_units(a[f"ffn{k}_w_up"][0], [block(j) for j in range(FT)])
        return np.stack([gate, upw], axis=1).reshape(2 * FT, P, UW)

    def down(k):
        w = square_units(a[f"ffn{k}_w_down"][0], [block(j) for j in range(KT)])
        return np.ascontiguousarray(w.reshape(KT, P, 2, DW).transpose(0, 2, 1, 3)).reshape(2 * KT, P, DW)

    at, start = {}, 0
    for name, width in (("aq", NH * HD), ("ak", P), ("av", P), ("hq", S), ("ff", S), ("fb", S), ("hi", S), ("hg", S),
                        ("ga", D), ("gb", D)):
        at[name] = start
        start += width
    head = np.arange(HD)

    def cols(kind, t):
        if kind == "aq":
            return at["aq"] + np.concatenate([HD * t + head, HD * (t + 4) + head])
        if kind == "hf":
            return np.concatenate([at["ff"] + HD * t + head, at["fb"] + HD * t + head])
        return at[kind] + block(t)

    w_in = a["w_in"][0]
    proj = square_units(w_in, [cols(kind, t) for kind, t in PROJ])
    pair_rows = np.concatenate([np.concatenate([HD * t + head, HD * (t + 4) + head]) for t in range(4)])
    branches = np.concatenate([a["w_branch_attn"][0][pair_rows], a["w_branch_hgrn"][0]], axis=0)
    branch = square_units(branches, [block(j) for j in range(KT)])
    gates = [square_units(w_in, [cols(g, j) for j in range(KT)]) for g in ("ga", "gb")]
    gates = np.stack(gates, axis=1).reshape(2 * KT, P, UW)
    wout = square_units(a["w_out"][0], [block(j) for j in range(KT)])

    def column_tiles(v):
        return v.reshape(-1, P).T

    gains = np.concatenate([column_tiles(a["ffn1_norm_g"][0]), column_tiles(a["mix_norm_g"][0]), column_tiles(a["ffn2_norm_g"][0]),
                            column_tiles(a["final_norm_g"]), np.concatenate([a["q_norm_g"][0]] * 2)[:, None],
                            np.concatenate([a["k_norm_g"][0]] * 2)[:, None], column_tiles(a["hgrn_out_norm_g"][0]),
                            (np.arange(P)[:, None] // CHUNK == np.arange(4)[None]).astype(np.float32)], axis=1)
    lb = a["hgrn_lb_logits"].reshape(2, 2, HH, HD).transpose(0, 3, 1, 2).reshape(P, 2, HH)

    grid_w, n_freq = 64, HD // 4
    inv = (np.float32(10000.0) ** (-np.arange(n_freq, dtype=np.float32) / np.float32(n_freq))).astype(np.float32)
    pos = np.arange(S)
    ang = np.concatenate([(pos // grid_w).astype(np.float32)[:, None] * inv, (pos % grid_w).astype(np.float32)[:, None] * inv], axis=1)
    p = np.arange(P)
    cos = np.cos(ang).astype(np.float32)[:, p % 32].T
    sin = np.sin(ang).astype(np.float32)[:, p % 32].T * np.where(p % HD < 32, -1.0, 1.0)[:, None]
    keep = np.where(p[:, None] < HD, pos[None] % CHUNK != 0, pos[None] % CHUNK != CHUNK - 1)
    same = p[:, None] // CHUNK == p[None] // CHUNK
    mask = np.concatenate([same & (p[:, None] <= p[None]), same & (p[:, None] >= p[None])], axis=1)
    swap = (p // HD * HD + (p % HD + 32) % HD)[:, None] == p[None]
    head_mean = (p[:, None] // HD == p[None] // HD) / HD
    consts = np.concatenate([cos, sin, keep, mask, head_mean, swap], axis=1).astype(np.float32)

    xT = a["x"][0].reshape(S, KT, P).transpose(2, 1, 0)
    arrays = {
        "xT": xT, "up1": up(1), "down1": down(1), "proj": proj, "gates": gates, "branch": branch, "wout": wout, "up2": up(2), "down2": down(2),
        "mix_const": consts, "small_const": np.concatenate([np.ones((P, P)), np.eye(P)], axis=1).astype(np.float32), "gains": gains, "lb_logits": lb,
    }
    arrays = {k: np.ascontiguousarray(v) for k, v in arrays.items()}
    nc = bacc.Bacc("TRN2", target_bir_lowering=False, num_devices=1)
    args = [nc.dram_tensor(f"{k}_dram", v.shape, F32, kind="ExternalInput").ap() for k, v in arrays.items()]
    out = nc.dram_tensor("outT_dram", (P, KT, S), F32, kind="ExternalOutput").ap()
    x_spill = nc.dram_tensor("x_spill_dram", (P, KT, S), F32, kind="Internal").ap()
    build(nc, *args, x_spill, out)
    got = run_bass_kernel_spmd(nc, [{f"{k}_dram": v for k, v in arrays.items()}], core_ids=[0]).results[0]["outT_dram"]
    return np.ascontiguousarray(np.asarray(got).transpose(2, 1, 0).reshape(1, S, D))
```

```python
from contextlib import ExitStack

import numpy as np

import concourse.bass as bass
from concourse import mybir

F32 = mybir.dt.float32
F32R = mybir.dt.float32r
I32 = mybir.dt.int32
U32 = mybir.dt.uint32
ALU = mybir.AluOpType
ACT = mybir.ActivationFunctionType
AX = mybir.AxisListType

P = 128
D, S, FF = 1024, 512, 2816
HD = 64
NH, NKV = 8, 2
HH = 8
CHUNK = 32
NCH = S // CHUNK
EPS = 1e-6
KT = D // P
FT = FF // P
ST = S // P
UW = KT * P
DW = FT // 2 * P
RAW_SLOTS, W_SLOTS, AHEAD = 2, 4, 3
PAIRS = HH // 2

STREAMS = [("up1", 2 * FT, UW), ("down1", 2 * KT, DW), ("proj", 26, UW), ("gates", 2 * KT, UW),
           ("branch", KT, UW), ("wout", KT, UW), ("up2", 2 * FT, UW), ("down2", 2 * KT, DW)]
BASE, WIDTH = {}, []
for _name, _count, _width in STREAMS:
    BASE[_name] = len(WIDTH)
    WIDTH += [_width] * _count
UNITS = len(WIDTH)

PROJ = ([("av", 0), ("ak", 0)] + [("aq", t) for t in range(4)] + [("hi", t) for t in range(4)]
        + [("hf", h) for h in range(4)] + [("hq", t) for t in range(4)]
        + [("hf", h) for h in range(4, HH)] + [("hg", t) for t in range(4)])
V_TILES = {i: w for w, i in enumerate(i for i, (kind, _) in enumerate(PROJ) if kind in ("av", "hi"))}
FIRST_ITEM = 9
ITEMS = 4 * ST

GATES_ATTN, GATES_TAIL, GATES_HEAD = [0, 1], [2, 3], [[4], [5], [6], [7], [8], [9], [10, 11], [12, 13]]
GATE_PLACES = ([("x", n) for n in range(5)] + [("hq", 0), ("hq", 1), ("hgate", 0), ("hq", 2), ("hgate", 1), ("hq", 3),
               ("k_in0", 0), ("hgate", 2), ("k_in1", 0), ("v_exp", 0), ("v_exp", 1)])
GATES_LAST = [14, 15]
GONE = -1e5

MIX_CONSTS = [("cos", S), ("sin", S), ("keep", S), ("mask", 2 * P), ("head_mean", P), ("swap", P)]
MIX_COLS = sum(w for _, w in MIX_CONSTS)


def build(nc, xT_in, up1, down1, proj, gates, branch, wout, up2, down2, mix_const, small_const, gains, lb_logits, x_spill, outT):
    with ExitStack() as ctx:
        def sb(name, shape, dt=F32):
            return ctx.enter_context(nc.sbuf_tensor(name, shape, dt))

        def sem(name):
            return ctx.enter_context(nc.semaphore(name))

        xT = sb("xT", [P, KT, S])
        h_hi, h_lo = sb("h_hi", [P, KT, S], F32R), sb("h_lo", [P, KT, S], F32R)
        raw = sb("raw", [P, RAW_SLOTS, DW])
        w_hi, w_lo = sb("w_hi", [P, W_SLOTS, DW], F32R), sb("w_lo", [P, W_SLOTS, DW], F32R)
        rs = sb("rs", [P, S])
        sq_sum = sb("sq_sum", [P, S])
        sq = sb("sq", [P, S])
        small = sb("small", [P, 2 * P])
        ones, ident = small[:, 0:P], small[:, P:2 * P]
        norm_v, norm_y, norm_t = (sb(n, [P, ST]) for n in ("norm_v", "norm_y", "norm_t"))
        gain = sb("gain", [P, 42])
        gq8 = sb("gq8", [P, 1])
        lbl = sb("lbl", [P, 2, HH])
        lb, one_minus_lb = sb("lb", [P, HH]), sb("one_minus_lb", [P, HH])
        lbt = sb("lbt", [P, 2, HH])
        neg_max, prob_sum = sb("neg_max", [P, ITEMS, 2]), sb("prob_sum", [P, ITEMS, 2])
        inv_sum = sb("inv_sum", [P, 2])
        b_mid = sb("b_mid", [P, NCH])
        b_last = sb("b_last", [P, NCH + 2])

        REGION = 96 * 1024
        region_at = -(-nc.sbuf_base // 32) * 32
        sb("region", [P, REGION // 4 + 8])
        ffn_words = 2 * FT * S

        def at(name, kib, shape, dt=F32):
            n = 4 * int(np.prod(shape[1:]))
            assert kib * 1024 + n <= REGION, name
            return nc.alloc_sbuf_tensor_at(name, shape, dt, offset=region_at + int(kib * 1024))

        assert ffn_words * 4 <= 88 * 1024
        g_hi, g_lo = at("g_hi", 0, [P, FT, S], F32R), at("g_lo", 44, [P, FT, S], F32R)
        gn, sg, un = at("gn", 88, [P, S]), at("sg", 90, [P, S]), at("un", 92, [P, S])

        forget = at("forget", 0, [P, HH, S])
        yb = at("yb", 0, [P, 2 * PAIRS, S], F32R)
        ya_hi, ya_lo = at("ya_hi", 16, [P, 4, S], F32R), at("ya_lo", 24, [P, 4, S], F32R)
        hq, hgate = at("hq", 32, [P, 4, S]), at("hgate", 40, [P, 4, S])
        v_h = at("v_h", 48, [P, ST, S])
        consts = at("consts", 56, [P, MIX_COLS])
        c = {}
        col = 0
        for name, width in MIX_CONSTS:
            c[name] = consts[:, col:col + width]
            col += width
        qk = at("qk", 64, [P, 5, S])
        v_a = at("v_a", 74, [P, ST, P])
        prob = at("prob", 76, [P, 2, S])
        prob_t = at("prob_t", 80, [P, 2, ST, P])
        y_nat = at("y_nat", 84, [P, 2, P])
        q_cos = prob
        v_tmp = at("v_tmp", 85, [P, S])
        q_sq, q_ms, q_rs, q_t = (at(n, 87 + 2 * i, [P, S]) for i, n in enumerate(("q_sq", "q_ms", "q_rs", "q_t")))
        silu_tmp = [q_sq, q_ms, q_rs, q_t]
        k_in = [at("k_in0", 64, [P, S]), sq_sum]
        b_cum = [at("b_cum0", 66, [P, S])[:], at("b_cum1", 68, [P, S])[:], xT[:, 5, :]]
        k_sc = [at("k_sc0", 70, [P, S]), at("k_sc1", 72, [P, S])]
        q_sc, k_end, q_dup = at("q_sc", 74, [P, S]), at("k_end", 76, [P, S]), at("q_dup", 78, [P, S])
        k_nat = sq
        sc_m = at("sc_m", 80, [P, 2, S])
        state = at("state", 84, [P, HD, NCH])
        decay = xT[:, 6:8, :].rearrange("p a b -> p (a b)")
        v_exp = at("v_exp", 88, [P, ST, HD, 4])
        o_ms, o_rs = at("o_ms", 92, [P, S]), at("o_rs", 94, [P, S])
        o_t = at("o_t", 56, [P, S])
        o_u = at("o_u", 58, [P, S])
        m_hi, m_lo = at("m_hi", 66, [P, KT, S], F32R), at("m_lo", 48, [P, KT, S], F32R)
        halves = v_exp[:].rearrange("p (i a) e c -> p i (a e c)", i=2)
        places = {"x": xT, "hq": hq, "hgate": hgate, "v_exp": halves, "k_in0": k_in[0][:].unsqueeze(1),
                  "k_in1": k_in[1][:].unsqueeze(1)}
        gate_at = [places[name][:, n, :] for name, n in GATE_PLACES]

        ps = ctx.enter_context(nc.psum_tensor("ps", [P, 8, S], F32))
        UP_BANKS, RES_BANKS, MEAN_BANK = (0, 2), 4, 6

        raw_loaded = [sem(f"raw_loaded{i}") for i in range(RAW_SLOTS)]
        x_loaded = [sem(f"x_loaded{n}") for n in range(KT)]
        const_loaded, small_loaded, mix_loaded = sem("const_loaded"), sem("small_loaded"), sem("mix_loaded")
        hi_done, lo_done, unit_done = sem("hi_done"), sem("lo_done"), sem("unit_done")
        x_done, sq_done, sum_done = sem("x_done"), sem("sq_done"), sem("sum_done")
        hh_done, h_done, mean_done = sem("hh_done"), sem("h_done"), sem("mean_done")
        diag_done, spread_done, rs_done = sem("diag_done"), sem("spread_done"), sem("rs_done")
        gate_read, up_read, sig_done = sem("gate_read"), sem("up_read"), sem("sig_done")
        prod_done, act_done, ghi_done, glo_done = sem("prod_done"), sem("act_done"), sem("ghi_done"), sem("glo_done")
        dve_seq, act_seq = sem("dve_seq"), sem("act_seq")
        lb_loaded, lb_exp, lb_ready = sem("lb_loaded"), sem("lb_exp"), sem("lb_ready")
        proj_read = sem("proj_read")
        vt_done, vn_done = sem("vt_done"), sem("vn_done")
        qsq_done, qms_done, qeps_done, qr_done = sem("qsq_done"), sem("qms_done"), sem("qeps_done"), sem("qr_done")
        cos_done = sem("cos_done")
        qn_done, qswap_done, rope_done = sem("qn_done"), sem("qswap_done"), sem("rope_done")
        s_done, nm_done, p_done, pt_done = sem("s_done"), sem("nm_done"), sem("p_done"), sem("pt_done")
        pta_done, ptb_done, pv_done, yn_done = sem("pta_done"), sem("ptb_done"), sem("pv_done"), sem("yn_done")
        yt_done, yahi_done, yalo_done = sem("yt_done"), sem("yahi_done"), sem("yalo_done")
        fs_done, sl_done, sil_done, dup_done = sem("fs_done"), sem("sl_done"), sem("sil_done"), sem("dup_done")
        f_done, k_done, lf_done = sem("f_done"), sem("k_done"), sem("lf_done")
        b_mid_done, to_end_done, b_last_done = sem("b_mid_done"), sem("to_end_done"), sem("b_last_done")
        decay_done = sem("decay_done")
        exp_q_done, exp_k_done, exp_end_done, exp_b_done = sem("exp_q_done"), sem("exp_k_done"), sem("exp_end_done"), sem("exp_b_done")
        qs_done, ks_done, ke_done, qe_done = sem("qs_done"), sem("ks_done"), sem("ke_done"), sem("qe_done")
        sc_done, scm_done, kt_done, kn_done = sem("sc_done"), sem("scm_done"), sem("kt_done"), sem("kn_done")
        zero_done, vexp_done, con_done, state_done = sem("zero_done"), sem("vexp_done"), sem("con_done"), sem("state_done")
        o_done, ocopy_done, osq_done, oms_done = sem("o_done"), sem("ocopy_done"), sem("osq_done"), sem("oms_done")
        oeps_done, or_done, on_done, ybhi_done, yblo_done = (sem(n) for n in (
            "oeps_done", "or_done", "on_done", "ybhi_done", "yblo_done"))
        spilled, x_back, sgate_done = sem("spilled"), sem("x_back"), sem("sgate_done")
        br_read, m_done, mhi_done, mlo_done = sem("br_read"), sem("m_done"), sem("mhi_done"), sem("mlo_done")
        scaled, out_dve, out_pool, out_stored = sem("scaled"), sem("out_dve"), sem("out_pool"), sem("out_stored")
        POOL_OUT = (5, 6, 7)
        RAW_CREDIT, W_CREDIT, BANK_CREDIT = RAW_SLOTS, W_SLOTS, 2

        block = ctx.enter_context(nc.Block())
        last = UNITS - 1

        @block.sync
        def _(sp):
            for name, count, width in STREAMS:
                src, base = dict(up1=up1, down1=down1, proj=proj, gates=gates, branch=branch, wout=wout, up2=up2, down2=down2)[name], BASE[name]
                with sp.Fori(0, count // 2) as it:
                    for i in range(2):
                        sp.wait_ge(lo_done, 2 * it + base + i + 1)
                        sp.dma_start(raw[:, i, 0:width], src[2 * it + i, :, :]).then_inc(raw_loaded[i], 16)
            for n in (0, 1, 5, 2, 3, 6, 4, 7):
                if n in POOL_OUT:
                    sp.wait_ge(out_pool, n - POOL_OUT[0] + 1)
                else:
                    sp.wait_ge(out_dve, n + 1)
                sp.dma_start(outT[:, n, :], xT[:, n, :]).then_inc(out_stored, 16)
            sp.wait_ge(out_stored, 16 * KT)

        @block.gpsimd
        def _(pool):
            def accumulate(first, n_of, a):
                pool.wait_ge(sq_done, a + 1)
                if a == 0:
                    pool.sem_inc(sum_done, 1)
                elif a < KT:
                    pool.wait_ge(sum_done, a)
                    nc.gpsimd.tensor_tensor(sq_sum[:], sq_sum[:], (sq, un)[a % 2][:], ALU.add).then_inc(sum_done, 1)
                elif first:
                    nc.gpsimd.tensor_copy(sq_sum[:], sq[:]).then_inc(sum_done, 1)
                else:
                    pool.wait_ge(sum_done, a)
                    nc.gpsimd.tensor_tensor(sq_sum[:], sq_sum[:], sq[:], ALU.add).then_inc(sum_done, 1)

            for r in range(2):
                if r:
                    pool.wait_ge(mean_done, r)
                for n in range(KT):
                    accumulate(n == 0, n, 8 * r + n)
            nc.gpsimd.memset(b_last[:], GONE).then_inc(zero_done, 1)
            pool.wait_ge(mix_loaded, 16)
            for m in range(5):
                pool.wait_ge(qn_done, m + 1)
                if m >= 2:
                    pool.wait_ge(rope_done, m - 1)
                nc.gpsimd.tensor_tensor(q_cos[:, m % 2, :], qk[:, m, :], c["cos"], ALU.mult).then_inc(cos_done, 1)

            def f_gate(h):
                pool.wait_ge(fs_done, h + 1)
                nc.gpsimd.tensor_scalar(forget[:, h, :], forget[:, h, :], one_minus_lb[:, h:h + 1], lb[:, h:h + 1],
                                        ALU.mult, ALU.add).then_inc(f_done, 1)

            def query(h):
                pool.wait_ge(exp_q_done, h + 1)
                pool.wait_ge(dup_done, h + 1)
                nc.gpsimd.tensor_tensor(q_sc[:], q_sc[:], q_dup[:], ALU.mult).then_inc(qs_done, 1)

            def key(h):
                pool.wait_ge(f_done, h + 1)
                if h == 0:
                    pool.wait_ge(s_done, 2 * ITEMS)
                if h >= 2:
                    pool.wait_ge(ks_done, h - 1)
                nc.gpsimd.tensor_scalar(k_in[h % 2][:], forget[:, h, :], -1.0, 1.0, ALU.mult, ALU.add).then_inc(k_done, 1)

            def to_end(h):
                pool.wait_ge(b_last_done, h + 1)
                if h == 0:
                    pool.wait_ge(pt_done, 2 * ITEMS)
                else:
                    pool.wait_ge(kt_done, h)
                chunks = lambda t: t.rearrange("p (n c) -> p n c", c=CHUNK)
                nc.gpsimd.tensor_tensor(chunks(k_end[:]), b_last[:, 1:NCH + 1].unsqueeze(2).to_broadcast([P, NCH, CHUNK]), chunks(b_cum[h % 3]),
                                        ALU.subtract).then_inc(to_end_done, 1)

            def key_to_end(h):
                pool.wait_ge(exp_end_done, h + 1)
                nc.gpsimd.tensor_tensor(k_end[:], k_end[:], k_in[h % 2][:], ALU.mult).then_inc(ke_done, 1)

            def value(h):
                if h >= 1:
                    pool.wait_ge(con_done, h)
                else:
                    pool.wait_ge(vn_done, 5)
                    pool.wait_ge(sil_done, HH)
                shape = [P, ST, HD, 4]
                nc.gpsimd.tensor_tensor(v_exp[:], v_h[:, :, HD * h:HD * (h + 1)].unsqueeze(3).to_broadcast(shape),
                                        gain[:, 38:42].unsqueeze(1).unsqueeze(1).to_broadcast(shape), ALU.mult).then_inc(vexp_done, 1)

            f_gate(0)
            key(0)
            pool.wait_ge(zero_done, 1)
            f_gate(1)
            key(1)
            to_end(0)
            pool.wait_ge(pv_done, ITEMS)
            nc.gpsimd.memset(sc_m[:], 0.0).then_inc(zero_done, 1)
            query(0)
            key_to_end(0)
            pool.wait_ge(vn_done, 5)
            pool.wait_ge(yt_done, ITEMS)
            nc.gpsimd.memset(state[:], 0.0).then_inc(zero_done, 1)
            value(0)
            to_end(1)
            for h in range(HH - 1):
                query(h + 1)
                key_to_end(h + 1)
                if h + 2 < HH:
                    f_gate(h + 2)
                    key(h + 2)
                value(h + 1)
                if h + 2 < HH:
                    to_end(h + 2)
            for r in range(2, 4):
                pool.wait_ge(mean_done, r)
                for n in range(KT if r < 3 else KT - 1):
                    accumulate(n == 0, n, 8 * r + n)
            for i, n in enumerate(POOL_OUT):
                pool.wait_ge(rs_done, 4)
                pool.wait_ge(scaled, n + 1)
                nc.gpsimd.tensor_tensor(xT[:, n, :], xT[:, n, :], rs[:], ALU.mult).then_inc(out_pool, 1)

        @block.scalar
        def _(act):
            A = nc.scalar.activation
            act.dma_start(gain[:], gains).then_inc(const_loaded, 16)
            nc.scalar.preload_act_table_set("sigmoid_and_others")
            for n in range(KT):
                act.dma_start(xT[:, n, :], xT_in[:, n, :]).then_inc(x_loaded[n], 16)
            act.dma_start(small[:], small_const).then_inc(small_loaded, 16)
            act.dma_start(lbl[:], lb_logits).then_inc(lb_loaded, 16)
            act.sem_inc(unit_done, W_CREDIT)

            def split_hi(cst, it=0, width=None):
                if isinstance(it, int):
                    if cst + 4 * it > last:
                        return
                    width = WIDTH[cst + 4 * it]
                act.wait_ge(raw_loaded[cst % 2], 16 * (cst // 2 + 1) + 32 * it)
                act.wait_ge(unit_done, cst + 1 + 4 * it)
                A(w_hi[:, cst % 4, 0:width], raw[:, cst % 2, 0:width], ACT.Copy).then_inc(hi_done, 1)

            def x_tile(r, it, q, split):
                n = 2 * it + q
                a = 8 * r + n
                act.wait_ge(x_done, 8 * (r - 1) + n + 1 + BANK_CREDIT)
                act.wait_ge(sum_done, a)
                A(sq[:], xT[:, n, :], ACT.Square).then_inc(sq_done, 1)
                if split:
                    A(h_hi[:, n, :], xT[:, n, :], ACT.Copy,
                      scale=gain[:, bass.ds(8 * r + n, 1)]).then_inc(hh_done, 1)
                if r == 3:
                    act.wait_ge(sq_done, a + 1)
                    A(xT[:, n, :], xT[:, n, :], ACT.Copy,
                      scale=gain[:, bass.ds(8 * r + n, 1)]).then_inc(scaled, 1)

            def ffn(k):
                base, f0 = BASE[f"up{k}"], FT * (k - 1)

                def up_body(it, static):
                    for q in range(2):
                        f = f0 + 2 * it + q
                        split_hi(base + 2 * q + AHEAD, it, UW)
                        split_hi(base + 2 * q + 1 + AHEAD, it, UW)
                        act.wait_ge(gate_read, f + 1 + BANK_CREDIT)
                        A(sg[:], gn[:], ACT.Sigmoid).then_inc(sig_done, 1)
                        act.wait_ge(act_done, f + 1)
                        A(g_hi[:, 2 * it + q, :], un[:], ACT.Copy).then_inc(ghi_done, 1)

                with act.Fori(0, FT // 2 - 1) as it:
                    up_body(it, False)
                up_body(FT // 2 - 1, True)
                base, r = BASE[f"down{k}"], 1 if k == 1 else 3

                def down_body(it):
                    for q in range(2):
                        for w in range(2):
                            split_hi(base + 2 * q + w + AHEAD, it, DW)
                        x_tile(r, it, q, split=k == 1)

                with act.Fori(0, KT // 2 - 1) as it:
                    down_body(it)
                down_body(KT // 2 - 1)

            act.wait_ge(const_loaded, 16)
            for n in range(KT):
                act.wait_ge(x_loaded[n], 16)
                A(h_hi[:, n, :], xT[:, n, :], ACT.Copy, scale=gain[:, n:n + 1]).then_inc(hh_done, 1)
                if n in (0, 4):
                    split_hi(n // 4)
            for n in range(KT):
                if n >= 3:
                    act.wait_ge(sum_done, n - 1)
                A((sq, un)[n % 2][:] if n else sq_sum[:], xT[:, n, :], ACT.Square).then_inc(sq_done, 1)
                if n == 2:
                    split_hi(2)
            ffn(1)

            def prob_t_copy(q):
                act.wait_ge(pt_done, 2 * q + 1)
                if q:
                    act.wait_ge(pv_done, q)
                A(prob_t[:, 0, :, :].rearrange("p a b -> p (a b)"), ps[:, 4, :], ACT.Copy).then_inc(pta_done, 1)

            def exp_scores(q):
                for a in range(2):
                    act.wait_ge(nm_done, 2 * q + 1 + a)
                    if q:
                        act.wait_ge(pt_done, 2 * q - 1 + a)
                    A(prob[:, a, :], ps[:, 2 + a, :], ACT.Exp, bias=neg_max[:, q, a:a + 1],
                      accum_out=prob_sum[:, q, a:a + 1]).then_inc(p_done, 1)

            def y_hi(t):
                act.wait_ge(yt_done, 4 * t + 4)
                A(ya_hi[:, t, :], ps[:, 7, :], ACT.Copy).then_inc(yahi_done, 1)

            def sigmoids():
                act.wait_ge(proj_read, len(PROJ) + BANK_CREDIT)
                for j in range(HH):
                    A(forget[:, j, :], forget[:, j, :], ACT.Sigmoid).then_inc(fs_done, 1)
                    if j >= 4:
                        act.wait_ge(sil_done, j - 3)
                    A(silu_tmp[j % 4][:], (hq, hgate)[j // 4][:, j % 4, :], ACT.Sigmoid).then_inc(sl_done, 1)
                nc.scalar.preload_act_table_set("natural_log_exp_and_others")

            act.dma_start(consts[:], mix_const).then_inc(mix_loaded, 16)
            act.wait_ge(h_done, 16)
            act.dma_start(x_spill, xT[:]).then_inc(spilled, 16)
            nc.scalar.preload_act_table_set("natural_log_exp_and_others")
            base = BASE["proj"]
            for i, (kind, t) in enumerate(PROJ):
                if i == 2:
                    act.wait_ge(lb_ready, 1)
                    A(lbt[:], lbt[:], ACT.Exp).then_inc(lb_exp, 1)
                if 3 <= i <= 7:
                    m = i - 3
                    act.wait_ge(qms_done, m + 1)
                    if m:
                        act.wait_ge(qn_done, m)
                    A(q_ms[:], ps[:, 4, :], ACT.Copy, bias=EPS).then_inc(qeps_done, 1)
                    act.wait_ge(qeps_done, m + 1)
                    A(q_rs[:], q_ms[:], ACT.Ln).then_inc(act_seq, 1)
                    act.wait_ge(act_seq, m + 1)
                    A(q_rs[:], q_rs[:], ACT.Exp, scale=-0.5).then_inc(qr_done, 1)
                for n in {0: (0, 1), 1: ()}.get(i, (i,)):
                    split_hi(base + n + AHEAD)
                if kind in ("ak", "aq"):
                    m = i - 1
                    act.wait_ge(proj_read, i + 1 + BANK_CREDIT)
                    if m:
                        act.wait_ge(qms_done, m)
                    A(q_sq[:], qk[:, m, :], ACT.Square).then_inc(qsq_done, 1)
                w = V_TILES.get(i - 1)
                if w is not None:
                    act.wait_ge(vt_done, w + 1)
                    vt = ps[:, 7, :].rearrange("p (a b) -> p a b", b=P)
                    A(v_a[:] if w == 0 else v_h[:, :, P * (w - 1):P * w], vt, ACT.Copy).then_inc(vn_done, 1)
                q = i - FIRST_ITEM
                if q >= 7 and q % 4 == 3:
                    y_hi(q // 4 - 1)
                if q >= 1:
                    prob_t_copy(q - 1)
                if 0 <= q < ITEMS:
                    exp_scores(q)
            gate_base = BASE["gates"]

            def log_f(h):
                act.wait_ge(f_done, h + 1)
                act.wait_ge(k_done, h + 1)
                A(forget[:, h, :], forget[:, h, :], ACT.Ln).then_inc(lf_done, 1)

            def exponentials(h):
                act.wait_ge(b_mid_done, h + 1)
                if h == 0:
                    act.wait_ge(pv_done, ITEMS)
                if h:
                    act.wait_ge(sc_done, h)
                A(q_sc[:], k_sc[h % 2][:], ACT.Exp).then_inc(exp_q_done, 1)
                act.wait_ge(exp_q_done, h + 1)
                A(k_sc[h % 2][:], k_sc[h % 2][:], ACT.Exp, scale=-1.0).then_inc(exp_k_done, 1)
                act.wait_ge(to_end_done, h + 1)
                A(k_end[:], k_end[:], ACT.Exp).then_inc(exp_end_done, 1)
                A(b_cum[h % 3], b_cum[h % 3], ACT.Exp).then_inc(exp_b_done, 1)

            def duplicate_q(h):
                if h:
                    act.wait_ge(qe_done, h)
                    act.wait_ge(qs_done, h)
                else:
                    act.wait_ge(pt_done, 2 * ITEMS)
                act.wait_ge(sil_done, h // 2 + 1)
                for rows in (slice(0, HD), slice(HD, P)):
                    ins = A(q_dup[rows, :], hq[slice(HD * (h % 2), HD * (h % 2) + HD), h // 2, :], ACT.Copy)
                ins.then_inc(dup_done, 1)

            def decays(h):
                if h:
                    act.wait_ge(state_done, h)
                else:
                    act.wait_ge(b_last_done, 1)
                for rows, first in ((slice(0, HD), 0), (slice(HD, P), 2)):
                    ins = A(decay[rows, :].rearrange("p (e n) -> p e n", n=NCH),
                            b_last[rows, first:first + NCH].unsqueeze(1).to_broadcast([HD, HD, NCH]), ACT.Exp)
                ins.then_inc(decay_done, 1)

            def norm_exp(t):
                act.wait_ge(oms_done, t + 1)
                A(o_ms[:], ps[:, 6, :], ACT.Copy, bias=EPS).then_inc(oeps_done, 1)
                act.wait_ge(oeps_done, t + 1)
                A(o_rs[:], o_ms[:], ACT.Ln).then_inc(act_seq, 1)
                act.wait_ge(act_seq, 5 + t + 1)
                A(o_rs[:], o_rs[:], ACT.Exp, scale=-0.5).then_inc(or_done, 1)

            def yb_hi(t):
                act.wait_ge(on_done, t + 1)
                A(yb[:, 2 * t, :], o_u[:], ACT.Copy).then_inc(ybhi_done, 1)

            def keys_to_sbuf(h):
                act.wait_ge(kt_done, h + 1)
                if h:
                    act.wait_ge(con_done, h)
                A(k_nat[:], ps[:, 6, :], ACT.Copy).then_inc(kn_done, 1)

            g0, g1 = GATES_ATTN
            g2, g3 = GATES_TAIL
            sigmoids()
            log_f(0)
            split_hi(gate_base + g0 + AHEAD)
            duplicate_q(0)
            split_hi(gate_base + g1 + AHEAD)
            exponentials(0)
            log_f(1)
            y_hi(3)
            split_hi(gate_base + g2 + AHEAD)
            act.wait_ge(spilled, 16)
            decays(0)
            split_hi(gate_base + g3 + AHEAD)
            keys_to_sbuf(0)
            duplicate_q(1)
            exponentials(1)
            for h in range(HH):
                for g in GATES_HEAD[h][:1]:
                    split_hi(gate_base + g + AHEAD)
                if h + 2 < HH:
                    log_f(h + 2)
                if h and h % 2 == 0:
                    norm_exp(h // 2 - 1)
                if h + 1 < HH:
                    decays(h + 1)
                    keys_to_sbuf(h + 1)
                if h + 2 < HH:
                    duplicate_q(h + 2)
                for g in GATES_HEAD[h][1:]:
                    split_hi(gate_base + g + AHEAD)
                if h + 2 < HH:
                    exponentials(h + 2)
                if h and h % 2 == 0:
                    yb_hi(h // 2 - 1)
                if h % 2:
                    act.wait_ge(ocopy_done, h // 2 + 1)
                    A(o_ms[:], o_t[:], ACT.Square).then_inc(osq_done, 1)
            split_hi(gate_base + GATES_LAST[0] + AHEAD)
            norm_exp(PAIRS - 1)
            yb_hi(PAIRS - 1)
            split_hi(gate_base + GATES_LAST[1] + AHEAD)

            base = BASE["branch"]
            for n in range(KT):
                split_hi(base + n + AHEAD)
                for g in (2 * n, 2 * n + 1):
                    if g == 0:
                        act.wait_ge(proj_read, len(PROJ) + 2 * KT + BANK_CREDIT)
                    A(gate_at[g], gate_at[g], ACT.Sigmoid).then_inc(sgate_done, 1)
                act.wait_ge(m_done, n + 1)
                A(m_hi[:, n, :], gate_at[2 * n], ACT.Copy).then_inc(mhi_done, 1)
                if n == 4:
                    act.wait_ge(mlo_done, 4)
                    act.wait_ge(spilled, 16)
                    act.dma_start(xT[:], x_spill).then_inc(x_back, 16)
            base = BASE["wout"]

            def wout_body(it):
                for q in range(4):
                    n = 4 * it + q
                    split_hi(base + q + AHEAD, it, UW)
                    x_tile(2, 2 * it, q, True)

            with act.Fori(0, 2) as it:
                wout_body(it)
            ffn(2)

        @block.vector
        def _(dve):
            V = nc.vector
            seq = [0]

            def link(ins):
                seq[0] += 1
                ins.then_inc(dve_seq, 1)
                dve.wait_ge(dve_seq, seq[0])

            def tt(out, a, b, op):
                return V.tensor_tensor(out, a, b, op)

            def stt(out, a, s, b, op0, op1):
                return V.scalar_tensor_tensor(out, a, s, b, op0, op1)

            def split_lo(cst, it=0, width=None):
                if isinstance(it, int):
                    if cst + 4 * it > last:
                        return
                    width = WIDTH[cst + 4 * it]
                dve.wait_ge(hi_done, cst + 1 + 4 * it)
                tt(w_lo[:, cst % 4, 0:width], raw[:, cst % 2, 0:width], w_hi[:, cst % 4, 0:width].bitcast(F32),
                   ALU.subtract).then_inc(lo_done, 1)

            def newton(y, v, tmp):
                link(tt(tmp, y, y, ALU.mult))
                link(stt(tmp, tmp, -0.5, v, ALU.mult, ALU.mult))
                return stt(y, tmp, 1.5, y, ALU.add, ALU.mult)

            def rms_factor(m):
                dve.wait_ge(mean_done, m + 1)
                link(V.tensor_scalar(norm_v[:], ps[:, MEAN_BANK, 0:ST], 1.0 / D, EPS, ALU.mult, ALU.add))
                link(V.tensor_scalar(norm_y[:].bitcast(I32), norm_v[:].bitcast(I32), -0.5, float(0x5F3759DF), ALU.mult, ALU.add))
                for _ in range(3):
                    link(newton(norm_y[:], norm_v[:], norm_t[:]))
                tt(sq[:].rearrange("p (a b) -> p a b", b=P), ident.unsqueeze(1).to_broadcast([P, ST, P]),
                   norm_y[:].unsqueeze(2).to_broadcast([P, ST, P]), ALU.mult).then_inc(diag_done, 1)

            def rms_rows(m):
                dve.wait_ge(spread_done, m + 1)
                V.tensor_copy(rs[:], ps[:, MEAN_BANK, :]).then_inc(rs_done, 1)
                dve.wait_ge(rs_done, m + 1)

            def h_tile(r, it, q):
                n = 2 * it + q
                dve.wait_ge(hh_done, 8 * r + n + 1)
                stt(h_lo[:, n, :], xT[:, n, :], gain[:, bass.ds(8 * r + n, 1)], h_hi[:, n, :].bitcast(F32),
                    ALU.mult, ALU.subtract).then_inc(h_done, 1)

            def residual(r, it, q, done, factor):
                n = 2 * it + q
                dve.wait_ge(unit_done, done)
                stt(xT[:, n, :], ps[:, RES_BANKS + q % 2, :], factor, xT[:, n, :], ALU.mult, ALU.add).then_inc(x_done, 1)

            def ffn(k):
                base, f0 = BASE[f"up{k}"], FT * (k - 1)

                def up_body(it, first=False):
                    for q in range(2):
                        f = f0 + 2 * it + q
                        c0 = base + 2 * q
                        split_lo(c0 + AHEAD, it, UW)
                        if first and q == 0:
                            rms_factor(0 if k == 1 else 2)
                            split_lo(c0 + 1 + AHEAD, it, UW)
                            rms_rows(0 if k == 1 else 2)
                        dve.wait_ge(unit_done, c0 + 4 * it + 1 + W_CREDIT)
                        tt(gn[:], ps[:, UP_BANKS[0] + q, :], rs[:], ALU.mult).then_inc(gate_read, 1)
                        if not (first and q == 0):
                            split_lo(c0 + 1 + AHEAD, it, UW)
                        dve.wait_ge(unit_done, c0 + 1 + 4 * it + 1 + W_CREDIT)
                        tt(un[:], ps[:, UP_BANKS[1] + q, :], rs[:], ALU.mult).then_inc(up_read, 1)
                        dve.wait_ge(up_read, f + 1 + BANK_CREDIT)
                        tt(un[:], un[:], gn[:], ALU.mult).then_inc(prod_done, 1)
                        dve.wait_ge(prod_done, f + 1)
                        dve.wait_ge(sig_done, f + 1)
                        tt(un[:], un[:], sg[:], ALU.mult).then_inc(act_done, 1)
                        dve.wait_ge(ghi_done, f + 1)
                        tt(g_lo[:, 2 * it + q, :], un[:], g_hi[:, 2 * it + q, :].bitcast(F32), ALU.subtract).then_inc(glo_done, 1)
                        dve.wait_ge(glo_done, f + 1)

                up_body(0, True)
                with dve.Fori(1, FT // 2 - 1) as it:
                    up_body(it)
                up_body(FT // 2 - 1)
                base, r = BASE[f"down{k}"], 1 if k == 1 else 3

                def down_body(it):
                    for q in range(2):
                        for w in range(2):
                            split_lo(base + 2 * q + w + AHEAD, it, DW)
                        residual(r, it, q, base + 2 * q + 1 + 4 * it + 1 + W_CREDIT, 0.5)
                        if k == 1:
                            h_tile(r, it, q)

                with dve.Fori(0, KT // 2 - 1) as it:
                    down_body(it)
                down_body(KT // 2 - 1)

            dve.sem_inc(lo_done, RAW_CREDIT)
            for s in (gate_read, up_read, x_done, proj_read, br_read):
                dve.sem_inc(s, BANK_CREDIT)
            for n in range(KT):
                h_tile(0, 0, n)
                if n in (0, 4):
                    split_lo(n // 4)
            split_lo(2)
            ffn(1)

            def y_lo(q):
                if q >= 7 and q % 4 == 3:
                    t = q // 4 - 1
                    dve.wait_ge(yahi_done, t + 1)
                    tt(ya_lo[:, t, :], ps[:, 7, :], ya_hi[:, t, :].bitcast(F32), ALU.subtract).then_inc(yalo_done, 1)

            def attention_step(q):
                if 0 <= q - 2 < ITEMS:
                    dve.wait_ge(pv_done, q - 1)
                    link(V.reciprocal(inv_sum[:], prob_sum[:, q - 2, :]))
                    if q - 2 >= 2:
                        dve.wait_ge(yt_done, q - 3)
                    for a in range(2):
                        cols = slice(HD * a, HD * (a + 1))
                        ins = V.tensor_scalar(y_nat[:, q % 2, cols], ps[:, 6, cols], inv_sum[:, a:a + 1], None, ALU.mult)
                    ins.then_inc(yn_done, 1)
                if 0 <= q - 1 < ITEMS:
                    dve.wait_ge(pt_done, 2 * q)
                    V.tensor_copy(prob_t[:, 1, :, :].rearrange("p a b -> p (a b)"), ps[:, 5, :]).then_inc(ptb_done, 1)
                if 0 <= q < ITEMS:
                    for a in range(2):
                        dve.wait_ge(s_done, 2 * q + 1 + a)
                        V.reduce_max(neg_max[:, q, a:a + 1], ps[:, 2 + a, :], AX.X, negate=True).then_inc(nm_done, 1)

            def lower_bound():
                dve.wait_ge(lb_loaded, 16)
                link(tt(lb[:], lbl[:, 0, :], lbl[:, 1, :], ALU.max))
                tt(lbt[:, 0, :], lbl[:, 0, :], lb[:], ALU.subtract)
                tt(lbt[:, 1, :], lbl[:, 1, :], lb[:], ALU.subtract).then_inc(lb_ready, 1)
                V.tensor_scalar(gq8[:], gain[:, 32:33], HD ** -0.5, None, ALU.mult)
                dve.wait_ge(lb_exp, 1)
                link(tt(lb[:], lbt[:, 0, :], lbt[:, 1, :], ALU.add))
                link(V.reciprocal(lb[:], lb[:]))
                link(tt(lb[:], lb[:], lbt[:, 0, :], ALU.mult))
                link(V.tensor_scalar(one_minus_lb[:], lb[:], -1.0, 1.0, ALU.mult, ALU.add))

            def silu(j):
                dve.wait_ge(sl_done, j + 1)
                dst = (hq, hgate)[j // 4][:, j % 4, :]
                tt(dst, dst, silu_tmp[j % 4][:], ALU.mult).then_inc(sil_done, 1)

            base = BASE["proj"]
            for i, (kind, t) in enumerate(PROJ):
                if i == 2:
                    lower_bound()
                if 3 <= i <= 7:
                    m = i - 3
                    dve.wait_ge(qr_done, m + 1)
                    link(newton(q_rs[:], q_ms[:], q_t[:]))
                    stt(qk[:, m, :], qk[:, m, :], gain[:, 33:34] if m == 0 else gq8[:], q_rs[:],
                        ALU.mult, ALU.mult).then_inc(qn_done, 1)
                    dve.wait_ge(qn_done, m + 1)
                if i != 1:
                    split_lo(base + i + AHEAD)
                if i == 0:
                    rms_factor(1)
                    split_lo(base + 1 + AHEAD)
                    rms_rows(1)
                y_lo(i - FIRST_ITEM)
                w = V_TILES.get(i)
                if w:
                    dve.wait_ge(vt_done, w)
                dst = {"av": v_tmp[:], "hi": v_tmp[:], "ak": qk[:, 0, :], "aq": qk[:, min(1 + t, 4), :], "hf": forget[:, t, :],
                       "hq": hq[:, t % 4, :], "hg": hgate[:, t % 4, :]}[kind]
                dve.wait_ge(unit_done, base + i + 1 + W_CREDIT)
                tt(dst, ps[:, i % 2, :], rs[:], ALU.mult).then_inc(proj_read, 1)
                if 4 <= i <= 8:
                    m = i - 4
                    dve.wait_ge(mix_loaded, 16)
                    dve.wait_ge(qswap_done, m + 1)
                    link(tt(q_t[:], ps[:, 5 - 2 * (m % 2), :], c["sin"], ALU.mult))
                    dve.wait_ge(cos_done, m + 1)
                    tt(qk[:, m, :], q_cos[:, m % 2, :], q_t[:], ALU.add).then_inc(rope_done, 1)
                    dve.wait_ge(rope_done, m + 1)
                attention_step(i - FIRST_ITEM)
            gate_base = BASE["gates"]

            def gate_lo(g):
                split_lo(gate_base + g + AHEAD)

            def gate_evac(g):
                if g == 0:
                    dve.wait_ge(spilled, 16)
                dve.wait_ge(unit_done, gate_base + g + 1 + W_CREDIT)
                tt(gate_at[g], ps[:, g % 2, :], rs[:], ALU.mult).then_inc(proj_read, 1)

            fwd, bwd = slice(0, HD), slice(HD, P)
            chunks = lambda t: t.rearrange("p (n c) -> p n c", c=CHUNK)

            def cumulate(h):
                b, par = b_cum[h % 3], h % 2
                dve.wait_ge(lf_done, h + 1)
                if h >= 3:
                    dve.wait_ge(o_done, h - 2)
                V.tensor_tensor_scan(b[fwd, :], c["keep"][fwd, :], forget[fwd, h, :], 0.0, ALU.mult, ALU.add)
                link(V.tensor_tensor_scan(b[bwd, ::-1], c["keep"][bwd, ::-1], forget[bwd, h, ::-1], 0.0, ALU.mult, ALU.add))
                if h:
                    dve.wait_ge(decay_done, h)
                    dve.wait_ge(to_end_done, h)
                b3 = chunks(b)
                V.tensor_copy(b_last[fwd, 1:NCH], b3[fwd, 0:NCH - 1, CHUNK - 1])
                V.tensor_copy(b_last[bwd, 2:NCH + 1], b3[bwd, 1:NCH, 0]).then_inc(b_last_done, 1)
                V.tensor_copy(b_mid[fwd, :], b3[fwd, :, CHUNK // 2 - 1])
                link(V.tensor_copy(b_mid[bwd, :], b3[bwd, :, CHUNK // 2]))
                tt(chunks(k_sc[par][:]), b3, b_mid[:].unsqueeze(2).to_broadcast([P, NCH, CHUNK]), ALU.subtract).then_inc(b_mid_done, 1)

            def normalize(t):
                dve.wait_ge(or_done, t + 1)
                link(newton(o_rs[:], o_ms[:], o_u[:]))
                link(stt(o_t[:], o_t[:], gain[:, 34 + t:35 + t], o_rs[:], ALU.mult, ALU.mult))
                tt(o_u[:], o_t[:], hgate[:, t, :], ALU.mult).then_inc(on_done, 1)
                dve.wait_ge(on_done, t + 1)

            def yb_lo(t):
                dve.wait_ge(ybhi_done, t + 1)
                tt(yb[:, 2 * t + 1, :], o_u[:], yb[:, 2 * t, :].bitcast(F32), ALU.subtract).then_inc(yblo_done, 1)
                dve.wait_ge(yblo_done, t + 1)

            def query_key(h):
                par = h % 2
                dve.wait_ge(exp_k_done, h + 1)
                tt(k_sc[par][:], k_sc[par][:], k_in[par][:], ALU.mult).then_inc(ks_done, 1)
                dve.wait_ge(exp_b_done, h + 1)
                dve.wait_ge(dup_done, h + 1)
                tt(b_cum[h % 3], b_cum[h % 3], q_dup[:], ALU.mult).then_inc(qe_done, 1)

            g0, g1 = GATES_ATTN
            dve.wait_ge(zero_done, 1)
            dve.wait_ge(s_done, 2 * ITEMS)
            gate_evac(g0)
            for j in range(3):
                silu(j)
            attention_step(ITEMS + 1)
            for j in range(3, HH):
                silu(j)
            cumulate(0)
            gate_lo(g0)
            gate_evac(g1)
            gate_lo(g1)
            attention_step(ITEMS + 2)
            y_lo(ITEMS + 3)
            attention_step(ITEMS + 3)
            query_key(0)
            for g in GATES_TAIL:
                gate_lo(g)
                gate_evac(g)
            cumulate(1)
            dve.wait_ge(zero_done, 3)
            for h in range(HH):
                par, t, r = h % 2, h // 2, h % 2
                if h:
                    dve.wait_ge(o_done, h)
                for d in range(2):
                    dve.wait_ge(sc_done, h + 1)
                    ins = V.copy_predicated(sc_m[:, d, :].rearrange("p (a b) -> p a b", b=P),
                                            c["mask"][:, P * d:P * (d + 1)].bitcast(U32).unsqueeze(1).to_broadcast([P, ST, P]),
                                            ps[:, 2 + d, :].rearrange("p (a b) -> p a b", b=P))
                ins.then_inc(scm_done, 1)
                if h + 1 < HH:
                    query_key(h + 1)
                if r and t:
                    yb_lo(t - 1)
                dve.wait_ge(con_done, h + 1)
                dve.wait_ge(decay_done, h + 1)
                con, flat, end = ps[:, 4:6, :].rearrange("p a b -> p (a b)"), state[:].rearrange("p e n -> p (e n)"), HD * NCH
                V.tensor_tensor_scan(flat[fwd, 1:end], decay[fwd, 1:end], con[fwd, 0:end - 1], 0.0, ALU.mult, ALU.add)
                V.tensor_tensor_scan(flat[bwd, 0:end - 1][:, ::-1], decay[bwd, 0:end - 1][:, ::-1], con[bwd, 1:end][:, ::-1], 0.0,
                                     ALU.mult, ALU.add).then_inc(state_done, 1)
                for g in GATES_HEAD[h][:1]:
                    gate_lo(g)
                    gate_evac(g)
                for g in GATES_HEAD[h][1:]:
                    gate_lo(g)
                if h + 2 < HH:
                    cumulate(h + 2)
                for g in GATES_HEAD[h][1:]:
                    gate_evac(g)
                if r == 0 and t:
                    normalize(t - 1)
                if r:
                    dve.wait_ge(o_done, h + 1)
                    V.tensor_copy(o_t[:], ps[:, 7, :]).then_inc(ocopy_done, 1)
            g0, g1 = GATES_LAST
            gate_lo(g0)
            gate_evac(g0)
            normalize(PAIRS - 1)
            yb_lo(PAIRS - 1)
            gate_evac(g1)
            gate_lo(g1)

            base = BASE["branch"]
            for n in range(KT):
                ga, gb, bank = gate_at[2 * n], gate_at[2 * n + 1], 2 * ((n + 1) % 2)
                split_lo(base + n + AHEAD)
                dve.wait_ge(unit_done, base + n + 1 + W_CREDIT)
                dve.wait_ge(sgate_done, 2 * n + 2)
                tt(ga, ps[:, bank, :], ga, ALU.mult)
                tt(gb, ps[:, bank + 1, :], gb, ALU.mult).then_inc(br_read, 1)
                dve.wait_ge(br_read, n + 1 + BANK_CREDIT)
                tt(ga, ga, gb, ALU.add).then_inc(m_done, 1)
                dve.wait_ge(mhi_done, n + 1)
                tt(m_lo[:, n, :], ga, m_hi[:, n, :].bitcast(F32), ALU.subtract).then_inc(mlo_done, 1)
            base = BASE["wout"]

            def wout_body(it):
                for q in range(4):
                    split_lo(base + q + AHEAD, it, UW)
                    residual(2, 2 * it, q, base + q + 4 * it + 1 + W_CREDIT, 1.0)
                    h_tile(2, 2 * it, q)

            dve.wait_ge(x_back, 16)
            with dve.Fori(0, 2) as it:
                wout_body(it)
            ffn(2)
            rms_factor(3)
            rms_rows(3)
            for n in range(POOL_OUT[0]):
                dve.wait_ge(scaled, n + 1)
                tt(xT[:, n, :], xT[:, n, :], rs[:], ALU.mult).then_inc(out_dve, 1)

        @block.tensor
        def _(pe):
            T = nc.tensor

            def product(bank, slot, tiles, moving_hi, moving_lo, first_wait=None, start=True, stop=True, off=0):
                for j in range(tiles):
                    if first_wait:
                        first_wait(j)
                    cols = slice(P * (off + j), P * (off + j + 1))
                    T.matmul(ps[:, bank, :], w_hi[:, slot, cols], moving_hi(j), start=start and j == 0, stop=False)
                    T.matmul(ps[:, bank, :], w_hi[:, slot, cols], moving_lo(j), start=False, stop=False)
                    ins = T.matmul(ps[:, bank, :], w_lo[:, slot, cols], moving_hi(j), start=False,
                                   stop=stop and j == tiles - 1)
                return ins

            def h_unit(bank, cst, wait=None):
                return product(bank, cst % 4, KT, lambda j: h_hi[:, j, :], lambda j: h_lo[:, j, :], wait)

            def h_wait(m):
                return lambda j: pe.wait_ge(h_done, 8 * m + j + 1)

            def mean(m):
                pe.wait_ge(sum_done, 8 * m + (8 if m < 3 else 7))
                if m == 0:
                    pe.wait_ge(small_loaded, 16)
                if m == 3:
                    pe.wait_ge(sq_done, 8 * m + 8)
                for j in range(ST):
                    cols = slice(P * j, P * (j + 1))
                    ins = T.matmul(ps[:, MEAN_BANK, j:j + 1], sq_sum[:, cols], ones[:, 0:1], start=True, stop=m < 3)
                    if m == 3:
                        ins = T.matmul(ps[:, MEAN_BANK, j:j + 1], sq[:, cols], ones[:, 0:1], start=False, stop=True)
                ins.then_inc(mean_done, 1)

            def spread(m):
                pe.wait_ge(diag_done, m + 1)
                T.matmul(ps[:, MEAN_BANK, :], ones, sq[:], start=True, stop=True).then_inc(spread_done, 1)

            def ffn(k):
                base, f0, m = BASE[f"up{k}"], FT * (k - 1), 2 * (k - 1)

                def up_body(it, first=False):
                    for q in range(2):
                        for w, read in ((0, gate_read), (1, up_read)):
                            cst = base + 2 * q + w
                            pe.wait_ge(lo_done, cst + 4 * it + 1 + RAW_CREDIT)
                            pe.wait_ge(read, f0 + 2 * it + q + 1)
                            wait = h_wait(m) if first and q == 0 and w == 0 else None
                            h_unit(UP_BANKS[w] + q, cst, wait).then_inc(unit_done, 1)
                            if first and 2 * q + w == (2 if m == 0 else 0):
                                mean(m)
                            if first and 2 * q + w == (3 if m == 0 else 1):
                                spread(m)

                up_body(0, True)
                with pe.Fori(1, FT // 2) as it:
                    up_body(it)
                base, r = BASE[f"down{k}"], 0 if k == 1 else 2

                def down_body(it, first=False):
                    for q in range(2):
                        pe.wait_ge(x_done, 8 * r + 2 * it + q + 1)
                        for w in range(2):
                            cst = base + 2 * q + w
                            pe.wait_ge(lo_done, cst + 4 * it + 1 + RAW_CREDIT)
                            wait = (lambda j: pe.wait_ge(glo_done, f0 + FT // 2 * w + j + 1)) if first and q == 0 else None
                            product(RES_BANKS + q, cst % 4, FT // 2, lambda j: g_hi[:, FT // 2 * w + j, :],
                                    lambda j: g_lo[:, FT // 2 * w + j, :], wait, start=w == 0, stop=w == 1).then_inc(unit_done, 1)

                down_body(0, True)
                with pe.Fori(1, KT // 2) as it:
                    down_body(it)

            ffn(1)

            base = BASE["proj"]

            def scores(q):
                t, qt = q // 4, q % 4
                if q == 0:
                    pe.wait_ge(rope_done, 5)
                for a in range(2):
                    if q:
                        pe.wait_ge(p_done, 2 * q - 1 + a)
                    rows = slice(HD * a, HD * (a + 1))
                    T.matmul(ps[:, 2 + a, :], qk[rows, 1 + t, P * qt:P * (qt + 1)], qk[rows, 0, :],
                             start=True, stop=True).then_inc(s_done, 1)

            def prob_transposes(q):
                for a, ev in ((0, pta_done), (1, ptb_done)):
                    pe.wait_ge(p_done, 2 * q + 1 + a)
                    if q:
                        pe.wait_ge(ev, q)
                    for j in range(ST):
                        ins = T.transpose(ps[:, 4 + a, P * j:P * (j + 1)], prob[:, a, P * j:P * (j + 1)], ident)
                    ins.then_inc(pt_done, 1)

            def weighted(q):
                if q:
                    pe.wait_ge(yn_done, q)
                pe.wait_ge(vn_done, 1)
                for a, ev in ((0, pta_done), (1, ptb_done)):
                    pe.wait_ge(ev, q + 1)
                    for j in range(ST):
                        ins = T.matmul(ps[:, 6, HD * a:HD * (a + 1)], prob_t[:, a, j, :], v_a[:, j, HD * a:HD * (a + 1)],
                                       start=j == 0, stop=j == ST - 1)
                ins.then_inc(pv_done, 1)

            def y_transpose(q):
                t, qt = q // 4, q % 4
                pe.wait_ge(yn_done, q + 1)
                if q == 0:
                    pe.wait_ge(vn_done, 5)
                if t and qt == 0:
                    pe.wait_ge(yalo_done, t)
                T.transpose(ps[:, 7, P * qt:P * (qt + 1)], y_nat[:, q % 2, :], ident).then_inc(yt_done, 1)

            def items(q):
                if 0 <= q - 3 < ITEMS:
                    y_transpose(q - 3)
                if 0 <= q - 2 < ITEMS:
                    weighted(q - 2)
                if 0 <= q - 1 < ITEMS:
                    prob_transposes(q - 1)
                if 0 <= q < ITEMS:
                    scores(q)

            for i, (kind, t) in enumerate(PROJ):
                cst = base + i
                pe.wait_ge(lo_done, cst + 1 + RAW_CREDIT)
                pe.wait_ge(proj_read, i + 1)
                h_unit(i % 2, cst, h_wait(1) if i == 0 else None).then_inc(unit_done, 1)
                if i == 0:
                    mean(1)
                if i == 1:
                    spread(1)
                    pe.wait_ge(mix_loaded, 16)
                w = V_TILES.get(i - 1)
                if w is not None:
                    pe.wait_ge(proj_read, i + BANK_CREDIT)
                    if w:
                        pe.wait_ge(vn_done, w)
                    for j in range(ST):
                        ins = T.transpose(ps[:, 7, P * j:P * (j + 1)], v_tmp[:, P * j:P * (j + 1)], ident)
                    ins.then_inc(vt_done, 1)
                if 2 <= i <= 6:
                    m = i - 2
                    pe.wait_ge(qsq_done, m + 1)
                    if m:
                        pe.wait_ge(qeps_done, m)
                    T.matmul(ps[:, 4, :], c["head_mean"], q_sq[:], start=True, stop=True).then_inc(qms_done, 1)
                if 3 <= i <= 7:
                    m = i - 3
                    pe.wait_ge(qn_done, m + 1)
                    if m >= 2:
                        pe.wait_ge(rope_done, m - 1)
                    T.matmul(ps[:, 5 - 2 * (m % 2), :], c["swap"], qk[:, m, :], start=True, stop=True).then_inc(qswap_done, 1)
                items(i - FIRST_ITEM)
            def gate_unit(g):
                cst = BASE["gates"] + g
                pe.wait_ge(lo_done, cst + 1 + RAW_CREDIT)
                pe.wait_ge(proj_read, len(PROJ) + g + 1)
                h_unit(g % 2, cst).then_inc(unit_done, 1)

            for q, g in zip(range(len(PROJ) - FIRST_ITEM, ITEMS + 3), GATES_ATTN):
                gate_unit(g)
                items(q)
            for g in GATES_TAIL:
                gate_unit(g)

            fwd, bwd = slice(0, HD), slice(HD, P)

            def mean_square(t):
                pe.wait_ge(osq_done, t + 1)
                pe.wait_ge(kn_done, min(2 * t + 3, HH))
                T.matmul(ps[:, 6, :], c["head_mean"], o_ms[:], start=True, stop=True).then_inc(oms_done, 1)

            def key_transposes(h):
                pe.wait_ge(ke_done, h + 1)
                if h >= 3 and h % 2:
                    pe.wait_ge(oeps_done, h // 2)
                if h:
                    pe.wait_ge(kn_done, h)
                for j in range(ST):
                    ins = T.transpose(ps[:, 6, P * j:P * (j + 1)], k_end[:, P * j:P * (j + 1)], ident)
                ins.then_inc(kt_done, 1)

            def chunk_scores(h):
                pe.wait_ge(qs_done, h + 1)
                pe.wait_ge(ks_done, h + 1)
                if h:
                    pe.wait_ge(scm_done, h)
                for d, rows in enumerate((fwd, bwd)):
                    for j in range(ST):
                        cols = slice(P * j, P * (j + 1))
                        ins = T.matmul(ps[:, 2 + d, cols], k_sc[h % 2][rows, cols], q_sc[rows, cols], start=True, stop=True)
                ins.then_inc(sc_done, 1)

            def contributions(h):
                pe.wait_ge(kn_done, h + 1)
                pe.wait_ge(vexp_done, h + 1)
                if h:
                    pe.wait_ge(state_done, h)
                for j in range(ST):
                    for half in range(2):
                        ins = T.matmul(ps[:, 4 + half, :].rearrange("p (e n) -> p e n", n=NCH)[:, :, 4 * j:4 * j + 4],
                                       k_nat[:, P * j:P * (j + 1)], v_exp[:, j, HD // 2 * half:HD // 2 * (half + 1), :],
                                       start=True, stop=True)
                ins.then_inc(con_done, 1)

            def outputs(h):
                pe.wait_ge(scm_done, h + 1)
                pe.wait_ge(qe_done, h + 1)
                pe.wait_ge(state_done, h + 1)
                if h % 2 == 0 and h:
                    pe.wait_ge(ocopy_done, h // 2)
                rows = slice(HD * (h % 2), HD * (h % 2 + 1))
                for j in range(ST):
                    v_t = v_h[:, j, HD * h:HD * (h + 1)]
                    cols = slice(P * j, P * (j + 1))
                    for d in range(2):
                        T.matmul(ps[rows, 7, cols], v_t, sc_m[:, d, cols], start=d == 0, stop=False)
                    for n in range(4 * j, 4 * j + 4):
                        cc = slice(CHUNK * n, CHUNK * (n + 1))
                        ins = T.matmul(ps[rows, 7, cc], state[:, :, n], b_cum[h % 3][:, cc], start=False, stop=n == 4 * j + 3)
                ins.then_inc(o_done, 1)

            key_transposes(0)
            chunk_scores(0)
            for h in range(HH):
                for g in GATES_HEAD[h][:1]:
                    gate_unit(g)
                if h and h % 2 == 0:
                    mean_square(h // 2 - 1)
                contributions(h)
                for g in GATES_HEAD[h][1:]:
                    gate_unit(g)
                if h + 1 < HH:
                    key_transposes(h + 1)
                    chunk_scores(h + 1)
                outputs(h)
            gate_unit(GATES_LAST[0])
            mean_square(PAIRS - 1)
            gate_unit(GATES_LAST[1])

            base = BASE["branch"]
            pe.wait_ge(yalo_done, 4)
            for n in range(KT):
                bank = 2 * ((n + 1) % 2)
                pe.wait_ge(lo_done, base + n + 1 + RAW_CREDIT)
                pe.wait_ge(br_read, n + 1)
                if n == 1:
                    pe.wait_ge(proj_read, len(PROJ) + 2 * KT + BANK_CREDIT)
                slot = (base + n) % 4
                product(bank, slot, 4, lambda j: ya_hi[:, j, :], lambda j: ya_lo[:, j, :])
                product(bank + 1, slot, 4, lambda j: yb[:, 2 * j, :], lambda j: yb[:, 2 * j + 1, :],
                        (lambda j: pe.wait_ge(yblo_done, j + 1)) if n == 0 else None, off=4).then_inc(unit_done, 1)
            base = BASE["wout"]

            def wout_body(it, first=False):
                for q in range(4):
                    cst = base + q
                    pe.wait_ge(lo_done, cst + 4 * it + 1 + RAW_CREDIT)
                    pe.wait_ge(x_done, 8 + 4 * it + q + 1)
                    wait = (lambda j: pe.wait_ge(mlo_done, j + 1)) if first and q == 0 else None
                    product(RES_BANKS + q % 2, cst % 4, KT, lambda j: m_hi[:, j, :], lambda j: m_lo[:, j, :], wait).then_inc(unit_done, 1)

            wout_body(0, True)
            wout_body(1)
            ffn(2)
            mean(3)
            spread(3)


def kernel(**inputs):
    import concourse.bacc as bacc
    from concourse.bass_utils import run_bass_kernel_spmd

    a = {k: np.asarray(v) for k, v in inputs.items()}

    def square_units(w, order):
        t = w.reshape(w.shape[0] // P, P, w.shape[1])
        return np.stack([np.ascontiguousarray(t[:, :, cols].transpose(1, 0, 2)).reshape(P, -1) for cols in order])

    def block(j):
        return np.arange(P * j, P * (j + 1))

    def up(k):
        gate = square_units(a[f"ffn{k}_w_gate"][0], [block(j) for j in range(FT)])
        upw = square_units(a[f"ffn{k}_w_up"][0], [block(j) for j in range(FT)])
        return np.stack([gate, upw], axis=1).reshape(2 * FT, P, UW)

    def down(k):
        w = square_units(a[f"ffn{k}_w_down"][0], [block(j) for j in range(KT)])
        return np.ascontiguousarray(w.reshape(KT, P, 2, DW).transpose(0, 2, 1, 3)).reshape(2 * KT, P, DW)

    at, start = {}, 0
    for name, width in (("aq", NH * HD), ("ak", P), ("av", P), ("hq", S), ("ff", S), ("fb", S), ("hi", S), ("hg", S),
                        ("ga", D), ("gb", D)):
        at[name] = start
        start += width
    head = np.arange(HD)

    def cols(kind, t):
        if kind == "aq":
            return at["aq"] + np.concatenate([HD * t + head, HD * (t + 4) + head])
        if kind == "hf":
            return np.concatenate([at["ff"] + HD * t + head, at["fb"] + HD * t + head])
        return at[kind] + block(t)

    w_in = a["w_in"][0]
    proj = square_units(w_in, [cols(kind, t) for kind, t in PROJ])
    pair_rows = np.concatenate([np.concatenate([HD * t + head, HD * (t + 4) + head]) for t in range(4)])
    branches = np.concatenate([a["w_branch_attn"][0][pair_rows], a["w_branch_hgrn"][0]], axis=0)
    branch = square_units(branches, [block(j) for j in range(KT)])
    gates = [square_units(w_in, [cols(g, j) for j in range(KT)]) for g in ("ga", "gb")]
    gates = np.stack(gates, axis=1).reshape(2 * KT, P, UW)
    wout = square_units(a["w_out"][0], [block(j) for j in range(KT)])

    def column_tiles(v):
        return v.reshape(-1, P).T

    gains = np.concatenate([column_tiles(a["ffn1_norm_g"][0]), column_tiles(a["mix_norm_g"][0]), column_tiles(a["ffn2_norm_g"][0]),
                            column_tiles(a["final_norm_g"]), np.concatenate([a["q_norm_g"][0]] * 2)[:, None],
                            np.concatenate([a["k_norm_g"][0]] * 2)[:, None], column_tiles(a["hgrn_out_norm_g"][0]),
                            (np.arange(P)[:, None] // CHUNK == np.arange(4)[None]).astype(np.float32)], axis=1)
    lb = a["hgrn_lb_logits"].reshape(2, 2, HH, HD).transpose(0, 3, 1, 2).reshape(P, 2, HH)

    grid_w, n_freq = 64, HD // 4
    inv = (np.float32(10000.0) ** (-np.arange(n_freq, dtype=np.float32) / np.float32(n_freq))).astype(np.float32)
    pos = np.arange(S)
    ang = np.concatenate([(pos // grid_w).astype(np.float32)[:, None] * inv, (pos % grid_w).astype(np.float32)[:, None] * inv], axis=1)
    p = np.arange(P)
    cos = np.cos(ang).astype(np.float32)[:, p % 32].T
    sin = np.sin(ang).astype(np.float32)[:, p % 32].T * np.where(p % HD < 32, -1.0, 1.0)[:, None]
    keep = np.where(p[:, None] < HD, pos[None] % CHUNK != 0, pos[None] % CHUNK != CHUNK - 1)
    same = p[:, None] // CHUNK == p[None] // CHUNK
    mask = np.concatenate([same & (p[:, None] <= p[None]), same & (p[:, None] >= p[None])], axis=1)
    swap = (p // HD * HD + (p % HD + 32) % HD)[:, None] == p[None]
    head_mean = (p[:, None] // HD == p[None] // HD) / HD
    consts = np.concatenate([cos, sin, keep, mask, head_mean, swap], axis=1).astype(np.float32)

    xT = a["x"][0].reshape(S, KT, P).transpose(2, 1, 0)
    arrays = {
        "xT": xT, "up1": up(1), "down1": down(1), "proj": proj, "gates": gates, "branch": branch, "wout": wout, "up2": up(2), "down2": down(2),
        "mix_const": consts, "small_const": np.concatenate([np.ones((P, P)), np.eye(P)], axis=1).astype(np.float32), "gains": gains, "lb_logits": lb,
    }
    arrays = {k: np.ascontiguousarray(v) for k, v in arrays.items()}
    nc = bacc.Bacc("TRN2", target_bir_lowering=False, num_devices=1)
    args = [nc.dram_tensor(f"{k}_dram", v.shape, F32, kind="ExternalInput").ap() for k, v in arrays.items()]
    out = nc.dram_tensor("outT_dram", (P, KT, S), F32, kind="ExternalOutput").ap()
    x_spill = nc.dram_tensor("x_spill_dram", (P, KT, S), F32, kind="Internal").ap()
    build(nc, *args, x_spill, out)
    got = run_bass_kernel_spmd(nc, [{f"{k}_dram": v for k, v in arrays.items()}], core_ids=[0]).results[0]["outT_dram"]
    return np.ascontiguousarray(np.asarray(got).transpose(2, 1, 0).reshape(1, S, D))
```
